# Optimizing a Trainium2 kernel written in Bass

```python
import jax, jax.numpy as jnp
from jax import lax
import numpy as np

D_MODEL = 2048
BATCH = 1
SEQ = 256
DEPTH = 1

N_MEM = 256
MLA_HEADS = 16
QK_NOPE_DIM = 128
QK_ROPE_DIM = 64
V_HEAD_DIM = 128
KV_LORA_RANK = 512
QK_HEAD_DIM = QK_NOPE_DIM + QK_ROPE_DIM
SOFTMAX_SCALE = QK_HEAD_DIM ** -0.5
ROPE_THETA = 10000.0
Q_BLOCK = 128
LRU_WIDTH = D_MODEL
LRU_BLOCKS = 16
LRU_BLOCK_DIM = LRU_WIDTH // LRU_BLOCKS
LRU_CONV_WIDTH = 4
LRU_C = 8.0
X_HEADS = 4
X_HEAD_DIM = 128
D_FF = 5632
FFN_CONV_WIDTH = 3
EPS = 1e-6

Q_COLS = MLA_HEADS * QK_HEAD_DIM
IN_SIZES = (Q_COLS, KV_LORA_RANK, QK_ROPE_DIM, LRU_WIDTH, LRU_WIDTH, D_MODEL, D_MODEL)
IN_COLS = sum(IN_SIZES)
IN_SPLIT_IDX = tuple(int(v) for v in np.cumsum(IN_SIZES)[:-1])

kernel_name = "hybrid_mla_rglru_gated_merge_layer"

def rmsnorm(x, g):
    x32 = x.astype(jnp.float32)
    y = x32 * lax.rsqrt(jnp.mean(x32 * x32, axis=-1, keepdims=True) + EPS)
    return (y * g.astype(jnp.float32)).astype(x.dtype)

def rope_tables(positions):
    inv_freq = ROPE_THETA ** (-jnp.arange(0, QK_ROPE_DIM, 2, dtype=jnp.float32) / QK_ROPE_DIM)
    ang = positions.astype(jnp.float32)[..., None] * inv_freq
    return jnp.cos(ang), jnp.sin(ang)

def apply_rope(x, cos, sin):
    x32 = x.astype(jnp.float32)
    x1, x2 = jnp.split(x32, 2, axis=-1)
    out = jnp.concatenate([x1 * cos - x2 * sin, x2 * cos + x1 * sin], axis=-1)
    return out.astype(x.dtype)

def causal_dwconv(x, w, b):
    k_width = w.shape[0]
    s = x.shape[1]
    xp = jnp.pad(x, ((0, 0), (k_width - 1, 0), (0, 0)))
    acc = b
    for k in range(k_width):
        acc = acc + xp[:, k:k + s] * w[k]
    return acc

def mla_attention(q_in, ckv, k_rope, positions, g_ckv, w_ukv):
    b, s, _ = q_in.shape
    cos, sin = rope_tables(positions)
    q = q_in.reshape(b, s, MLA_HEADS, QK_HEAD_DIM)
    q_nope, q_rope = q[..., :QK_NOPE_DIM], q[..., QK_NOPE_DIM:]
    q_rope = apply_rope(q_rope, cos[:, :, None], sin[:, :, None])
    q = jnp.concatenate([q_nope, q_rope], axis=-1)
    k_rope = apply_rope(k_rope, cos, sin)
    kv = (rmsnorm(ckv, g_ckv) @ w_ukv).reshape(b, s, MLA_HEADS, QK_NOPE_DIM + V_HEAD_DIM)
    k_nope, v = kv[..., :QK_NOPE_DIM], kv[..., QK_NOPE_DIM:]
    k = jnp.concatenate([k_nope, jnp.broadcast_to(k_rope[:, :, None], (b, s, MLA_HEADS, QK_ROPE_DIM))], axis=-1)
    n_blocks = s // Q_BLOCK
    q_blocks = q.reshape(b, n_blocks, Q_BLOCK, MLA_HEADS, QK_HEAD_DIM).transpose(1, 0, 2, 3, 4)
    starts = jnp.arange(n_blocks, dtype=jnp.int32) * Q_BLOCK
    k_idx = jnp.arange(s, dtype=jnp.int32)

    def one_block(args):
        qb, start = args
        sc = jnp.einsum('bqhd,bkhd->bhqk', qb, k).astype(jnp.float32) * SOFTMAX_SCALE
        q_idx = start + jnp.arange(Q_BLOCK, dtype=jnp.int32)
        mask = q_idx[:, None] >= k_idx[None, :]
        p = jax.nn.softmax(jnp.where(mask, sc, -jnp.inf), axis=-1)
        return jnp.einsum('bhqk,bkhd->bqhd', p.astype(v.dtype), v)

    o = lax.map(one_block, (q_blocks, starts))
    return o.transpose(1, 0, 2, 3, 4).reshape(b, s, MLA_HEADS * V_HEAD_DIM)

def rg_lru(x, w_rg, b_rg, w_ig, b_ig, lam):
    b, s, w = x.shape
    xh = x.reshape(b, s, LRU_BLOCKS, LRU_BLOCK_DIM)
    r = jax.nn.sigmoid(jnp.einsum('bshi,hij->bshj', xh, w_rg) + b_rg).reshape(b, s, w)
    i = jax.nn.sigmoid(jnp.einsum('bshi,hij->bshj', xh, w_ig) + b_ig).reshape(b, s, w)
    log_a = -LRU_C * r.astype(jnp.float32) * jax.nn.softplus(-lam.astype(jnp.float32))
    a = jnp.exp(log_a)
    u = jnp.sqrt(-jnp.expm1(2.0 * log_a)) * (i * x).astype(jnp.float32)

    def combine(left, right):
        a1, b1 = left
        a2, b2 = right
        return a1 * a2, a2 * b1 + b2

    _, h = lax.associative_scan(combine, (a, u), axis=1)
    return h.astype(x.dtype)

def setup_inputs(seed: int = 0) -> dict:
    key = jax.random.key(seed)
    ks = jax.random.split(key, 32)
    f32 = jnp.float32

    def nrm(k, shape, fan_in):
        return jax.random.normal(k, shape, f32) * (fan_in ** -0.5)

    def gain(k, shape):
        return 1.0 + 0.05 * jax.random.normal(k, shape, f32)

    def bias(k, shape):
        return 0.01 * jax.random.normal(k, shape, f32)

    L = DEPTH
    x = jax.random.normal(ks[0], (BATCH, SEQ, D_MODEL), f32)
    mem = jax.random.normal(ks[1], (BATCH, N_MEM, D_MODEL), f32)
    offset = jax.random.randint(ks[2], (BATCH, 1), 0, 1024, dtype=jnp.int32)
    positions = offset + jnp.arange(SEQ, dtype=jnp.int32)[None, :]
    a0 = jax.random.uniform(ks[3], (L, LRU_WIDTH), f32, 0.9, 0.999)
    sig = a0 ** (1.0 / LRU_C)
    lru_lambda = jnp.log(sig) - jnp.log1p(-sig)
    return {
        "x": x,
        "mem": mem,
        "positions": positions,
        "g_pre_mix": gain(ks[4], (L, D_MODEL)),
        "g_post_mix": gain(ks[5], (L, D_MODEL)),
        "w_in": nrm(ks[6], (L, D_MODEL, IN_COLS), D_MODEL),
        "g_ckv": gain(ks[7], (L, KV_LORA_RANK)),
        "w_ukv": nrm(ks[8], (L, KV_LORA_RANK, MLA_HEADS * (QK_NOPE_DIM + V_HEAD_DIM)), KV_LORA_RANK),
        "w_o_mla": nrm(ks[9], (L, MLA_HEADS * V_HEAD_DIM, D_MODEL), MLA_HEADS * V_HEAD_DIM),
        "w_conv_lru": nrm(ks[10], (L, LRU_CONV_WIDTH, LRU_WIDTH), LRU_CONV_WIDTH),
        "b_conv_lru": bias(ks[11], (L, LRU_WIDTH)),
        "w_rg": nrm(ks[12], (L, LRU_BLOCKS, LRU_BLOCK_DIM, LRU_BLOCK_DIM), LRU_BLOCK_DIM),
        "b_rg": bias(ks[13], (L, LRU_BLOCKS, LRU_BLOCK_DIM)),
        "w_ig": nrm(ks[14], (L, LRU_BLOCKS, LRU_BLOCK_DIM, LRU_BLOCK_DIM), LRU_BLOCK_DIM),
        "b_ig": bias(ks[15], (L, LRU_BLOCKS, LRU_BLOCK_DIM)),
        "lru_lambda": lru_lambda,
        "w_o_lru": nrm(ks[16], (L, LRU_WIDTH, D_MODEL), LRU_WIDTH),
        "w_out": nrm(ks[17], (L, D_MODEL, D_MODEL), D_MODEL),
        "g_pre_x": gain(ks[18], (L, D_MODEL)),
        "g_post_x": gain(ks[19], (L, D_MODEL)),
        "g_mem": gain(ks[20], (L, D_MODEL)),
        "w_cq": nrm(ks[21], (L, D_MODEL, X_HEADS * X_HEAD_DIM), D_MODEL),
        "w_ck": nrm(ks[22], (L, D_MODEL, X_HEADS * X_HEAD_DIM), D_MODEL),
        "w_cv": nrm(ks[23], (L, D_MODEL, X_HEADS * X_HEAD_DIM), D_MODEL),
        "w_co": nrm(ks[24], (L, X_HEADS * X_HEAD_DIM, D_MODEL), X_HEADS * X_HEAD_DIM),
        "g_pre_ffn": gain(ks[25], (L, D_MODEL)),
        "g_post_ffn": gain(ks[26], (L, D_MODEL)),
        "w_up": nrm(ks[27], (L, D_MODEL, 2 * D_FF), D_MODEL),
        "w_fconv": nrm(ks[28], (L, FFN_CONV_WIDTH, 2 * D_FF), FFN_CONV_WIDTH),
        "b_fconv": bias(ks[29], (L, 2 * D_FF)),
        "w_down": nrm(ks[30], (L, D_FF, D_MODEL), D_FF),
    }

def reference(x, mem, positions, g_pre_mix, g_post_mix, w_in, g_ckv, w_ukv, w_o_mla,
              w_conv_lru, b_conv_lru, w_rg, b_rg, w_ig, b_ig, lru_lambda, w_o_lru, w_out,
              g_pre_x, g_post_x, g_mem, w_cq, w_ck, w_cv, w_co,
              g_pre_ffn, g_post_ffn, w_up, w_fconv, b_fconv, w_down):
    b, s, _ = x.shape
    m = mem.shape[1]
    for l in range(DEPTH):
        h = rmsnorm(x, g_pre_mix[l])
        proj = h @ w_in[l]
        q_in, ckv, k_rope, lru_x, lru_y, gate_mla, gate_lru = jnp.split(proj, IN_SPLIT_IDX, axis=-1)
        o_mla = mla_attention(q_in, ckv, k_rope, positions, g_ckv[l], w_ukv[l]) @ w_o_mla[l]
        xc = causal_dwconv(lru_x, w_conv_lru[l], b_conv_lru[l])
        hr = rg_lru(xc, w_rg[l], b_rg[l], w_ig[l], b_ig[l], lru_lambda[l])
        o_lru = (hr * jax.nn.gelu(lru_y, approximate=True)) @ w_o_lru[l]
        merged = jax.nn.sigmoid(gate_mla) * o_mla + jax.nn.sigmoid(gate_lru) * o_lru
        x = x + rmsnorm(merged @ w_out[l], g_post_mix[l])
        h = rmsnorm(x, g_pre_x[l])
        mn = rmsnorm(mem, g_mem[l])
        cq = (h @ w_cq[l]).reshape(b, s, X_HEADS, X_HEAD_DIM)
        ck = (mn @ w_ck[l]).reshape(b, m, X_HEADS, X_HEAD_DIM)
        cv = (mn @ w_cv[l]).reshape(b, m, X_HEADS, X_HEAD_DIM)
        sc = jnp.einsum('bshd,bmhd->bhsm', cq, ck).astype(jnp.float32) * (X_HEAD_DIM ** -0.5)
        p = jax.nn.softmax(sc, axis=-1).astype(cv.dtype)
        co = jnp.einsum('bhsm,bmhd->bshd', p, cv).reshape(b, s, X_HEADS * X_HEAD_DIM)
        x = x + rmsnorm(co @ w_co[l], g_post_x[l])
        h = rmsnorm(x, g_pre_ffn[l])
        up = causal_dwconv(h @ w_up[l], w_fconv[l], b_fconv[l])
        gate, val = jnp.split(up, 2, axis=-1)
        x = x + rmsnorm((jax.nn.gelu(gate, approximate=True) * val) @ w_down[l], g_post_ffn[l])
    return x


_drawn_inputs = setup_inputs


def setup_inputs(seed=0):
    import zlib

    import numpy as np

    out = dict(_drawn_inputs(seed))
    spreads = {}
    factors = {'b_rg': 36.962, 'b_ig': 8.0, 'b_fconv': 8.0}
    for name, (base, spread) in spreads.items():
        noise = np.random.default_rng([zlib.crc32(name.encode()), seed]).standard_normal(out[name].shape)
        drawn = base * np.exp(spread * noise) if base else spread * noise
        out[name] = __import__('jax').numpy.asarray(drawn.astype(out[name].dtype))
    for name, factor in factors.items():
        out[name] = (out[name] * factor).astype(out[name].dtype)
    return out
```

```python
from contextlib import ExitStack

import concourse.bass as bass
from concourse import mybir

F32 = mybir.dt.float32
F32R = mybir.dt.float32r
I32 = mybir.dt.int32
ALU = mybir.AluOpType
ACT = mybir.ActivationFunctionType
AX = mybir.AxisListType.X

P = 128
D = 2048
T = 256
KT = D // P
HEADS, NOPE, ROPE = 16, 128, 64
QH = NOPE + ROPE
RANK = 512
RT = RANK // P
XH = 4
DFF = 5632
FT = DFF // P
GROUPS = [(0, 16), (16, 16), (32, 12)]
EPS = 1e-6
SLOTS = 4
LEAD = 2
OFF_CKV = HEADS * QH
OFF_LX = OFF_CKV + RANK + ROPE
OFF_LY = OFF_LX + D
OFF_GM = OFF_LY + D
OFF_GL = OFF_GM + D
TWO_PI = (6.28125, 0.0019350051879882812, 3.019916050561733e-07)
MAGIC = 12582912.0
PI = 3.141592653589793
SCALE = QH ** -0.5
XSCALE = 128 ** -0.5
Q_ORDER = [1, 2, 0]
GELU_C = 1.5957691216057308
NEG = -1e30

G_PRE_MIX, G_POST_MIX, G_PRE_X, G_POST_X, G_MEM, G_PRE_FFN, G_POST_FFN, B_CONV = range(0, 128, 16)
W_CONV, B_RG, B_IG, LAM, G_CKV = 128, 192, 208, 224, 240
W_F, B_F = 256, 640


class Phase:

    def __init__(self, after, trips, ends):
        self.trips, self.ends, self.n = trips, ends, len(ends)
        self.p0 = after.p_end if after else 0
        self.t0 = after.t_end if after else 0
        self.g0 = after.g_end if after else 0
        self.used, self.done, g = [], [], 0
        for e in ends:
            self.done += [g + j + 1 for j in range(e)]
            g += max(e, 1)
            self.used.append(g)
        self.steps, self.tiles = g, sum(ends)
        self.p_end = self.p0 + self.n * trips
        self.t_end = self.t0 + self.tiles * trips
        self.g_end = self.g0 + self.steps * trips
        assert self.n % SLOTS == 0

    def p(self, i, c):
        return i * self.n + self.p0 + c

    def t(self, i, j):
        return i * self.tiles + self.t0 + j

    def g(self, i, off):
        return i * self.steps + self.g0 + off

    def landed(self, i, c):
        return i * (16 * self.n // SLOTS) + 16 * ((self.p0 + c) // SLOTS + 1)


class Tally:

    def __init__(self, eng, sem):
        self.eng, self.sem, self.n, self.off = eng, sem, 0, 0

    def mark(self, ins):
        ins.then_inc(self.sem, 1)
        self.n += 1
        return ins

    def now(self):
        return self.off + self.n

    def wait(self):
        self.eng.wait_ge(self.sem, self.now())

    def link(self, ins):
        self.mark(ins)
        self.wait()


PH_A = Phase(None, 1, [0] * 7 + [5])
PH_Q0 = Phase(PH_A, 1, [0, 0, 0, 3])
PH_UKV = Phase(PH_Q0, 2, [4] * 4)
PH_Q = Phase(PH_UKV, HEADS // 2 - 1, [0, 0, 0, 3])
PH_GM = Phase(PH_Q, 4, [0, 2, 0, 2])
PH_OM = Phase(PH_GM, 4, [0, 2, 0, 2])
PH_LRU = Phase(PH_OM, 8, [0, 2, 0, 2])
PH_OL = Phase(PH_LRU, 8, [0, 2, 0, 2])
PH_WO = Phase(PH_OL, 4, [0, 2, 0, 2])
PH_CK = Phase(PH_WO, 1, [0, 2, 0, 2])
PH_CV = Phase(PH_CK, 1, [0, 2, 0, 2])
PH_CQ = Phase(PH_CV, 1, [0, 2, 0, 2])
PH_CO = Phase(PH_CQ, 1, [4] * 4)
PH_UP, PH_DN, _last = [], [], PH_CO
for _first, _count in GROUPS:
    PH_UP.append(Phase(_last, _count // 2, [0, 2, 0, 2]))
    PH_DN.append(Phase(PH_UP[-1], KT // 4, [1] * 4))
    _last = PH_DN[-1]
PIECES = _last.p_end


def build(nc, a, out):
    def w3(ap):
        return ap.rearrange("(k p) c -> p k c", p=P)

    w_in, w_ukv, w_om, w_ol, w_out = (w3(a[n][0]) for n in ("w_in", "w_ukv", "w_o_mla", "w_o_lru", "w_out"))
    w_ck, w_cv, w_cq, w_co = (w3(a[n][0]) for n in ("w_ck", "w_cv", "w_cq", "w_co"))
    w_up, w_dn = w3(a["w_up"][0]), w3(a["w_down"][0])
    w_rg = a["w_rg"][0].rearrange("b i j -> i b j")
    w_ig = a["w_ig"][0].rearrange("b i j -> i b j")
    x_tok = a["x"][0].rearrange("(m p) d -> p m d", p=P)
    mem_tok = a["mem"][0].rearrange("(m p) d -> p m d", p=P)
    out_tok = out[0].rearrange("(m p) d -> p m d", p=P)

    with ExitStack() as ctx:
        def sb(name, shape, dt=F32):
            return ctx.enter_context(nc.sbuf_tensor(name, shape, dt))

        def sem(name):
            return ctx.enter_context(nc.semaphore(name))

        raw = sb("raw", [P, SLOTS, 2048])
        wsp = sb("wsp", [P, SLOTS, 2, 2048], F32R)
        hsp = sb("hsp", [P, KT, 2 * T], F32R)
        asp = sb("asp", [P, KT, 2 * T], F32R)
        big_a = sb("big_a", [P, KT, T])
        big_b = sb("big_b", [P, KT, T])
        scr = sb("scr", [P, 4096])
        cr = sb("cr", [P, 4, T])
        par = sb("par", [P, 6 * P])
        ident = sb("ident", [P, P])
        ones = sb("ones", [P, P])
        rotm = sb("rotm", [P, P])
        mask = sb("mask", [P, 3 * P])
        pos_i = sb("pos_i", [P, T], I32)
        invf = sb("invf", [P, 1])
        cur = sb("cur", [P, 512])
        st = sb("st", [P, 96])
        ps = ctx.enter_context(nc.psum_tensor("ps", [P, 8, 512], F32))

        def s(c, n=1):
            return scr[:, c * T:(c + n) * T]

        a_tok = big_a[:, :, :].rearrange("p (m k) t -> p m (k t)", m=2)
        b_tok = big_b[:, :, :].rearrange("p (m k) t -> p m (k t)", m=2)
        out_sb = raw[:, 0:2, :]
        PROW = scr[:, 0:6 * P].rearrange("p (t c) -> p t c", c=P)
        CKV = [s(j) for j in range(RT)]
        KRAW, KR, COS, SIN = s(4), s(5), s(6), s(7)
        RV, RS = s(8), s(9)
        SQ = [s(10 + j) for j in range(4)]
        PR = [scr[:, 384 * e:384 * e + 384] for e in range(2)]
        PT = [scr[:, 2048 + 384 * e:2048 + 384 * e + 384] for e in range(2)]
        QRAW, QROPE, ROTT = s(11), s(12), s(13)
        QN = [s(14), s(15)]
        VC = scr[:, 768:1280].rearrange("p (m e d) -> p m e d", m=2, e=2)
        KC = [cur[:, e * T:(e + 1) * T] for e in range(2)]
        GW = cur[:, :].rearrange("p (g e j) -> p g e j", g=2, e=2)
        XR, XC, RG, IG = ([s(n), s(n + 1)] for n in (0, 2, 4, 6))
        TH, SQT, RC, YY = ([s(n), s(n + 1)] for n in (8, 10, 12, 14))
        OL_O, OL_G = [s(0), s(1)], [s(2), s(3)]
        CVT = scr[:, 0:4 * T].rearrange("p (m d) -> p m d", m=2)
        CKT = [s(12 + j) for j in range(4)]
        ACC, ACS = s(4), [s(5), s(6)]
        RT0, RR = s(10), s(11)
        CQ = [big_a[:, j, :] for j in range(XH)]
        XP = [big_a[:, 4 + 2 * e:6 + 2 * e, :] for e in range(2)]
        XPT = [big_a[:, 8 + 2 * e:10 + 2 * e, :] for e in range(2)]
        UR, UC = [s(0), s(1), s(4), s(5)], [s(2), s(3), s(6), s(7)]
        HID = [s(12), s(13)]

        landed = [sem(f"landed{n}") for n in range(SLOTS)]
        hi_done, lo_done, gemm_step = sem("hi_done"), sem("lo_done"), sem("gemm_step")
        cross_done, tile_out = sem("cross_done"), sem("tile_out")
        dve_self, act_self, pool_self, pe_aux = sem("dve_self"), sem("act_self"), sem("pool_self"), sem("pe_aux")
        x_in, par_in, pos_in, gate_w_in, mem_in, x2_in = (
            sem(n) for n in ("x_in", "par_in", "pos_in", "gate_w_in", "mem_in", "x2_in"))
        out_stored = sem("out_stored")
        consts_made, prow_zero, mask_made = sem("consts_made"), sem("prow_zero"), sem("mask_made")
        lam_exp, kv_cur, y_sq = sem("lam_exp"), sem("kv_cur"), sem("y_sq")
        par_turned, par_ready = sem("par_turned"), sem("par_ready")
        x_sq, x_scaled, x_turned, x_hi, x_lo = (sem(n) for n in ("x_sq", "x_scaled", "x_turned", "x_hi", "x_lo"))
        x_root = sem("x_root")
        ckv_sq, ckv_sum, ckv_norm, ckv_hi, ckv_lo = (
            sem(n) for n in ("ckv_sq", "ckv_sum", "ckv_norm", "ckv_hi", "ckv_lo"))
        var_ready, root_ready = sem("var_ready"), sem("root_ready")
        angle_ready, table_ready = sem("angle_ready"), sem("table_ready")
        rot_done, roped = sem("rot_done"), sem("roped")
        scores_done, neg_max, exps_done, sums_inv, probs_ready, probs_turned, probs_copied, pv_done, o_hi, o_lo = (
            sem(n) for n in ("scores_done", "neg_max", "exps_done", "sums_inv", "probs_ready", "probs_turned",
                             "probs_copied", "pv_done", "o_hi", "o_lo"))
        gate_done = sem("gate_done")
        conv_done, gates_mm, gates_act, lru_t, lru_root, lru_a, lru_scan, y_poly, y_sig, hrg, hrg_hi, hrg_lo = (
            sem(n) for n in ("conv_done", "gates_mm", "gates_act", "lru_t", "lru_root", "lru_a", "lru_scan",
                             "y_poly", "y_sig", "hrg", "hrg_hi", "hrg_lo"))
        lru_rc, lru_u = sem("lru_rc"), sem("lru_u")
        olg_sig, merged_out, m_hi, m_lo = sem("olg_sig"), sem("merged_out"), sem("m_hi"), sem("m_lo")
        mem_sq, mem_root, mem_scaled, mem_turned, mem_hi, mem_lo = (
            sem(n) for n in ("mem_sq", "mem_root", "mem_scaled", "mem_turned", "mem_hi", "mem_lo"))
        ysq_done, norm_sum, rms_ready = sem("ysq_done"), sem("norm_sum"), sem("rms_ready")
        y_scaled, xt_turned, res_out, res_sq, res_hi, res_lo = (
            sem(n) for n in ("y_scaled", "xt_turned", "res_out", "res_sq", "res_hi", "res_lo"))
        up_ready, up_bias, up_conv, gelu_done, hid_out, hid_hi, hid_lo = (
            sem(n) for n in ("up_ready", "up_bias", "up_conv", "gelu_done", "hid_out", "hid_hi", "hid_lo"))
        fin_turned, fin_copied = sem("fin_turned"), sem("fin_copied")

        def xst(h, n):
            at = 64 + 8 * (h % 2) + 2 * n
            return st[:, at:at + 2]

        def col(base, m):
            return par[:, bass.ds(m + base, 1)]

        def piece_size(ph, c):
            if ph is PH_A:
                return 2 * (RANK + ROPE) if c < ph.n else 8 * QH
            if ph is PH_Q0 and c < ph.n:
                return 8 * QH
            return 2048

        block = ctx.enter_context(nc.Block())

        def rounds(eng, ph, body, last_apart=False):
            n = ph.trips - last_apart
            if n == 1:
                body(0)
            else:
                with eng.Fori(0, n) as i:
                    body(i)
            if last_apart:
                body(ph.trips - 1)

        @block.sync
        def _(sp):
            def piece(ph, i, c, k, cols, src):
                if not isinstance(i, int) or ph.p(i, c) >= SLOTS:
                    sp.wait_ge(lo_done, ph.p(i, c) - SLOTS + 1)
                slot = (ph.p0 + c) % SLOTS
                dst = raw[:, slot, 0:k * cols].rearrange("p (k c) -> p k c", k=k)
                sp.dma_start(dst, src).then_inc(landed[slot], 16)

            def wide(ph, i, c, w, col):
                h = KT // 2
                piece(ph, i, c, h, T, w[:, (c % 2) * h:(c % 2) * h + h, bass.ds(col, T)])

            def plain(ph, w, base=0):
                def body(i):
                    for c in range(4):
                        wide(ph, i, c, w, i * 512 + base + (c // 2) * T)
                rounds(sp, ph, body)

            def q_cols(ph, unit0):
                def body(i):
                    for c in range(4):
                        piece(ph, i, c, 4, 2 * QH, w_in[:, 4 * c:4 * c + 4, bass.ds(i * (2 * QH) + unit0 * 2 * QH, 2 * QH)])
                rounds(sp, ph, body)

            for c in range(8):
                piece(PH_A, 0, c, 2, RANK + ROPE, w_in[:, 2 * c:2 * c + 2, OFF_CKV:OFF_LX])
            q_cols(PH_Q0, 0)

            def ukv(i):
                for c in range(4):
                    piece(PH_UKV, i, c, RT, 512, w_ukv[:, :, bass.ds(i * 2048 + c * 512, 512)])
            rounds(sp, PH_UKV, ukv)
            q_cols(PH_Q, 1)
            plain(PH_GM, w_in, OFF_GM)
            plain(PH_OM, w_om)

            def lru(i):
                for c in range(4):
                    wide(PH_LRU, i, c, w_in, i * T + (OFF_LX if c < 2 else OFF_LY))
            rounds(sp, PH_LRU, lru)

            def o_lru(i):
                for c in range(4):
                    wide(PH_OL, i, c, w_ol if c < 2 else w_in, i * T + (0 if c < 2 else OFF_GL))
            rounds(sp, PH_OL, o_lru)
            plain(PH_WO, w_out)
            plain(PH_CK, w_ck)
            plain(PH_CV, w_cv)
            plain(PH_CQ, w_cq)
            for c in range(4):
                piece(PH_CO, 0, c, 4, 512, w_co[:, :, c * 512:(c + 1) * 512])
            for (f0, fn), up, dn in zip(GROUPS, PH_UP, PH_DN):
                def up_cols(i):
                    for c in range(4):
                        wide(up, i, c, w_up, i * T + f0 * P + (0 if c < 2 else DFF))
                rounds(sp, up, up_cols)

                def dn_cols(i):
                    for c in range(4):
                        piece(dn, i, c, fn, P, w_dn[:, f0:f0 + fn, bass.ds(i * 512 + c * P, P)])
                rounds(sp, dn, dn_cols)
            for kq in range(4):
                sp.wait_ge(fin_copied, 2 * kq + 2)
                cols = slice(kq * 512, (kq + 1) * 512)
                sp.dma_start(out_tok[:, :, cols], out_sb[:, :, cols]).then_inc(out_stored, 16)
            sp.wait_ge(out_stored, 64)

        @block.tensor
        def _(pe):
            last_in = {}

            def enter(ph, banks):
                need = max([last_in[b] + 1 for n, b in enumerate(banks)
                            if b in last_in and last_in[b] > ph.t0 + n - len(banks)] or [0])
                if need:
                    pe.wait_ge(tile_out, need)
                for n, b in enumerate(banks):
                    last_in[b] = ph.t_end - len(banks) + n

            def claim(ph, i, j, back=4):
                if not isinstance(i, int) or ph.t(i, j) >= back:
                    pe.wait_ge(tile_out, ph.t(i, j) + 1 - back)

            def arrive(ph, i, c):
                pe.wait_ge(lo_done, ph.p(i, c) + 1)

            def feature_tile(ph, i, c, j, bank, slot, lhs, k0, kn, src, first, last, note):
                for k in range(kn):
                    x = src[:, k0 + k, :]
                    f, l = first and k == 0, last and k == kn - 1
                    parts = [1, 0] if l and not f else [0, 1]
                    for n, part in enumerate(parts):
                        w = T if part else 2 * T
                        mm = pe.matmul(ps[:, bank, 0:w], lhs(part, k), x[:, 0:w], start=(f and part == 0),
                                       stop=(l and n == 1))
                if note:
                    mm.then_inc(gemm_step, 1)

            def token_tile(ph, bank, m, rhs, k0, kn, src, first, last, note):
                for k in range(kn):
                    f, l = first and k == 0, last and k == kn - 1
                    parts = [1, 0] if l and not f else [0, 1]
                    for n, part in enumerate(parts):
                        x = src[:, k0 + k, part * T + m * P:part * T + m * P + P]
                        if part:
                            o, r = ps[:, bank, 0:T], rhs(k, False)
                        else:
                            o, r = ps[:, bank, :], rhs(k, True)
                        mm = pe.matmul(o, x, r, start=(f and part == 0), stop=(l and n == 1))
                if note:
                    mm.then_inc(gemm_step, 1)

            def wtile(slot, part, kn, k, c0, cn=P):
                return wsp[:, slot, part, 0:2048 // kn * kn].rearrange("p (k c) -> p k c", k=kn)[:, k, c0:c0 + cn]

            def wide_unit(ph, i, u, src, between=None, ready=None):
                for h in range(2):
                    c = 2 * u + h
                    arrive(ph, i, c)
                    for j in range(2):
                        if h == 0:
                            claim(ph, i, 2 * u + j)
                        for k in range(8):
                            if ready and j == 0:
                                ready(8 * h + k)
                            f, l = h == 0 and k == 0, h == 1 and k == 7
                            feature_tile(ph, i, c, 2 * u + j, 2 * u + j, c, lambda part, _, k=k, j=j: wtile(c, part, 8, k, j * P),
                                         8 * h + k, 1, src, f, l, l or (h == 0 and j == 1 and k == 7))
                    if between:
                        between(c)

            def plain(ph, src):
                enter(ph, [0, 1, 2, 3])

                def body(i):
                    for u in range(2):
                        wide_unit(ph, i, u, src)
                rounds(pe, ph, body)

            pe.wait_ge(consts_made, 4)
            pe.wait_ge(par_in, 16 * 17)
            for n in range(6):
                mm = pe.transpose(ps[:, 4 + n // 4, (n % 4) * P:(n % 4 + 1) * P], PROW[:, n, :], ident[:, :])
                mm.then_inc(par_turned, 1)

            def turn(src_tok, k, bank, col, done):
                for m in range(2):
                    mm = pe.transpose(ps[:, bank, col + m * P:col + (m + 1) * P], src_tok[:, m, k * P:(k + 1) * P], ident[:, :])
                mm.then_inc(done, 1)

            pe.wait_ge(x_scaled, 2)
            pe.wait_ge(par_ready, 2)
            for k in range(KT):
                turn(a_tok, k, k // 2, (k % 2) * T, x_turned)

            for c in range(8):
                arrive(PH_A, 0, c)
                slot = c % SLOTS
                wv = [wsp[:, slot, part, 0:2 * (RANK + ROPE)].rearrange("p (k c) -> p k c", k=2) for part in range(2)]
                for k in range(2):
                    pe.wait_ge(x_lo, 2 * c + k + 1)
                for j in range(5):
                    if c == 0:
                        pe.wait_ge(x_lo, 2 * j + 2)
                    for k in range(2):
                        def lhs(part, _, k=k, j=j):
                            at = min(j * P, RANK + ROPE - P)
                            return wv[part][:, k, at:at + P]
                        f, l = c == 0 and k == 0, c == 7 and k == 1
                        feature_tile(PH_A, 0, c, j, j, slot, lhs, 2 * c + k, 1, hsp, f, l, l or (c < 7 and j == 4 and k == 1))

            def q_piece(ph, i, c):
                arrive(ph, i, c)
                for n, j in enumerate(Q_ORDER):
                    if c == 0:
                        claim(ph, i, n, 3)

                    def lhs(part, k):
                        w = wsp[:, c % SLOTS, part, 0:8 * QH].rearrange("p (k c) -> p k c", k=4)
                        return w[:, k, j * P:(j + 1) * P]
                    feature_tile(ph, i, c, n, j, c % SLOTS, lhs, 4 * c, 4, hsp, c == 0, c == 3, c == 3 or n == 2)

            def ckv_stats():
                pe.wait_ge(ckv_sq, RT)
                for j in range(RT):
                    mm = pe.matmul(ps[:, 5, 0:T], ones[:, :], SQ[j], start=(j == 0), stop=(j == RT - 1))
                mm.then_inc(ckv_sum, 1)
                pe.wait_ge(tile_out, 5)
                pe.matmul(ps[:, 6, 0:T], rotm[:, :], KRAW, start=True, stop=True).then_inc(rot_done, 1)

            for j in range(5):
                last_in[j] = j
            enter(PH_Q0, Q_ORDER)
            q_piece(PH_Q0, 0, 0)
            ckv_stats()
            for c in range(1, 4):
                q_piece(PH_Q0, 0, c)

            def ukv(i):
                for c in range(4):
                    arrive(PH_UKV, i, c)
                    wv = [wsp[:, c, part, :].rearrange("p (k e c) -> p k e c", k=RT, e=2) for part in range(2)]
                    for j in range(2):
                        claim(PH_UKV, i, 4 * c + j)
                        feature_tile(PH_UKV, i, c, j, j, c, lambda part, k: wv[part][:, k, j, 0:P], 0, RT, asp,
                                     True, True, True)
                    both = wsp[:, c, :, :].rearrange("p h (k e c) -> p h k e c", k=RT, e=2)
                    for m in range(2):
                        claim(PH_UKV, i, 4 * c + 2 + m)

                        def rhs(k, two):
                            return both[:, :, k, :, P:2 * P] if two else wv[0][:, k, :, P:2 * P]
                        token_tile(PH_UKV, 2 + m, m, rhs, 0, RT, asp, True, True, True)
            pe.wait_ge(ckv_lo, RT)
            enter(PH_UKV, [0, 1, 2, 3])
            rounds(pe, PH_UKV, ukv)

            def attention(u, qpiece):
                pe.wait_ge(tile_out, PH_Q.t(u, 0) - 1)
                pe.wait_ge(roped, u + 1)
                if not isinstance(u, int) or u:
                    pe.wait_ge(o_lo, u)
                pe.matmul(ps[:, 6, 0:T], rotm[:, :], QRAW, start=True, stop=True).then_inc(rot_done, 1)
                if qpiece:
                    qpiece(0)
                pe.wait_ge(roped, u + 2)
                pe.wait_ge(kv_cur, u * 2 + 2)
                for e in range(2):
                    rope = slice(64 * e, 64 * e + 64)
                    for q in range(2):
                        kn = P * (q + 1)
                        o = ps[:, 3 + e, P * q:P * q + kn]
                        pe.matmul(o, QN[e][:, q * P:(q + 1) * P], KC[e][:, 0:kn], start=True, stop=False)
                        mm = pe.matmul(o, QROPE[rope, q * P:(q + 1) * P], KR[rope, 0:kn], start=False, stop=True)
                    mm.then_inc(scores_done, 1)
                if qpiece:
                    qpiece(1)
                    qpiece(2)
                for e in range(2):
                    pe.wait_ge(probs_ready, u * 4 + 2 * e + 2)
                    for b in range(3):
                        mm = pe.transpose(ps[:, 5 + 2 * e, b * P:(b + 1) * P], PR[e][:, b * P:(b + 1) * P], ident[:, :])
                    mm.then_inc(probs_turned, 1)
                if qpiece:
                    qpiece(3)
                for e in range(2):
                    pe.wait_ge(probs_copied, u * 2 + e + 1)
                    o = ps[:, 6, e * T:(e + 1) * T]
                    pe.matmul(o, VC[:, 0, e, :], PT[e][:, 0:2 * P], start=True, stop=False)
                    mm = pe.matmul(o[:, P:2 * P], VC[:, 1, e, :], PT[e][:, 2 * P:3 * P], start=False, stop=True)
                mm.then_inc(pv_done, 1)

            enter(PH_Q, Q_ORDER)
            pe.wait_ge(tile_out, PH_UKV.t_end)
            rounds(pe, PH_Q, lambda i: attention(i, lambda c: q_piece(PH_Q, i, c)))
            attention(HEADS // 2 - 1, None)

            plain(PH_GM, hsp)
            pe.wait_ge(o_lo, HEADS // 2)
            plain(PH_OM, asp)

            enter(PH_LRU, [0, 1, 2, 3])

            def lru(i):
                def gates(c):
                    if c != 2:
                        return
                    pe.wait_ge(gate_w_in, i * 32 + 32)
                    for e in range(2):
                        pe.wait_ge(conv_done, i * 2 + e + 1)
                        pe.wait_ge(gates_act, i * 4 + 2 * e)
                        for g in range(2):
                            mm = pe.matmul(ps[:, 4 + e, g * T:(g + 1) * T], GW[:, g, e, :], XC[e], start=True, stop=True)
                        mm.then_inc(gates_mm, 1)
                wide_unit(PH_LRU, i, 0, hsp)
                wide_unit(PH_LRU, i, 1, hsp, between=gates)
            rounds(pe, PH_LRU, lru)

            enter(PH_OL, [0, 1, 2, 3])
            pe.wait_ge(hrg_lo, KT)

            def o_lru(i):
                wide_unit(PH_OL, i, 0, asp)
                wide_unit(PH_OL, i, 1, hsp)
            rounds(pe, PH_OL, o_lru)

            enter(PH_WO, [0, 1, 2, 3])
            pe.wait_ge(mem_scaled, 2)
            for k in range(8):
                turn(b_tok, k, 4 + k // 2, (k % 2) * T, mem_turned)

            def mem_rest(c):
                if c == 0:
                    for k in range(8, KT):
                        if k % 2 == 0:
                            pe.wait_ge(mem_lo, k - 6)
                        turn(b_tok, k, k // 2, (k % 2) * T, mem_turned)

            def m_ready(k):
                if k % 2 == 0:
                    pe.wait_ge(m_lo, k // 2 + 1)
            wide_unit(PH_WO, 0, 0, hsp, between=mem_rest, ready=m_ready)
            wide_unit(PH_WO, 0, 1, hsp)
            with pe.Fori(1, PH_WO.trips) as i:
                for u in range(2):
                    wide_unit(PH_WO, i, u, hsp)

            def norm(count):
                pe.wait_ge(ysq_done, count)
                pe.matmul(ps[:, 4, 0:T], ones[:, :], ACC, start=True, stop=True).then_inc(norm_sum, 1)

            res_at = {(0, 1): (0, 2), (0, 2): (2, 5), (0, 3): (5, 8), (1, 0): (8, 11), (1, 1): (11, 14), (1, 2): (14, 16)}

            def turn_x(ph_n, c):
                for k in range(*res_at.get((ph_n, c), (0, 0))):
                    if k == 0:
                        pe.wait_ge(x2_in, 16)
                    if k >= 3:
                        pe.wait_ge(res_out, k - 2)
                    turn(a_tok, k, 5 + k % 3, 0, xt_turned)

            def ck_between(c):
                if c == 0:
                    norm(KT)
                turn_x(0, c)
            enter(PH_CK, [0, 1, 2, 3])
            pe.wait_ge(mem_lo, KT)
            for u in range(2):
                wide_unit(PH_CK, 0, u, asp, between=ck_between)

            enter(PH_CV, [0, 1, 2, 3])
            for c in range(4):
                arrive(PH_CV, 0, c)
                u, h = c // 2, c % 2
                for m in range(2):
                    if h == 0:
                        claim(PH_CV, 0, 2 * u + m)

                    def rhs(k, two):
                        both = wsp[:, c, :, :].rearrange("p h (k c) -> p h k c", k=8)
                        return both[:, :, k, :] if two else both[:, 0, k, :]
                    for k in range(8):
                        f, l = h == 0 and k == 0, h == 1 and k == 7
                        token_tile(PH_CV, 2 * u + m, m, lambda _, two, k=k: rhs(k, two), 8 * h + k, 1, asp, f, l,
                                   l or (h == 0 and m == 1 and k == 7))
                turn_x(1, c)

            norm(2 * KT)
            pe.wait_ge(res_lo, KT)
            plain(PH_CQ, hsp)

            def x_scores(h):
                pe.wait_ge(tile_out, PH_CQ.t_end)
                if h == 0:
                    pe.wait_ge(rms_ready, 5)
                if h >= 2:
                    pe.wait_ge(exps_done, 32 + 2 * (h - 1))
                for q in range(2):
                    mm = pe.matmul(ps[:, 4 + h % 2, q * T:(q + 1) * T], CQ[h][:, q * P:(q + 1) * P], CKT[h],
                                   start=True, stop=True)
                mm.then_inc(scores_done, 1)
            x_scores(0)
            x_scores(1)
            for h in range(XH):
                pe.wait_ge(probs_ready, 32 + 2 * (h + 1))
                if h:
                    pe.wait_ge(probs_copied, HEADS + h)
                for m in range(2):
                    for q in range(2):
                        mm = pe.transpose(ps[:, 6, m * T + q * P:m * T + (q + 1) * P],
                                          XP[h % 2][:, q, m * P:(m + 1) * P], ident[:, :])
                mm.then_inc(probs_turned, 1)
                if h + 2 < XH:
                    x_scores(h + 2)
                pe.wait_ge(probs_copied, HEADS + h + 1)
                if h:
                    pe.wait_ge(o_lo, HEADS // 2 + h)
                for m in range(2):
                    mm = pe.matmul(ps[:, 7, 0:T], CVT[:, m, h * P:(h + 1) * P], XPT[h % 2][:, m, :],
                                   start=(m == 0), stop=(m == 1))
                mm.then_inc(pv_done, 1)

            enter(PH_CO, [0, 1, 2, 3])
            pe.wait_ge(o_lo, HEADS // 2 + XH)
            for c in range(4):
                arrive(PH_CO, 0, c)
                for j in range(4):
                    claim(PH_CO, 0, 4 * c + j)
                    feature_tile(PH_CO, 0, c, 4 * c + j, j, c, lambda part, k: wtile(c, part, 4, k, j * P),
                                 0, XH, asp, True, True, True)
            norm(3 * KT)

            for n, ((f0, fn), up, dn) in enumerate(zip(GROUPS, PH_UP, PH_DN)):
                enter(up, [0, 1, 2, 3])

                def up_round(i, first=False):
                    def x2_sum(c):
                        if c == 1:
                            norm(4 * KT)

                    def x2_ready(k):
                        pe.wait_ge(res_lo, KT + k + 1)
                    wide_unit(up, i, 0, hsp, between=x2_sum if first else None, ready=x2_ready if first else None)
                    wide_unit(up, i, 1, hsp)
                if n == 0:
                    up_round(0, True)
                    with pe.Fori(1, up.trips) as i:
                        up_round(i)
                else:
                    rounds(pe, up, up_round)

                enter(dn, [0, 1, 2, 3])

                def dn_round(i):
                    for c in range(4):
                        arrive(dn, i, c)
                        claim(dn, i, c)
                        for k in range(fn):
                            if c == 0 and k in (0, fn - 2):
                                pe.wait_ge(hid_lo, f0 + fn - (2 if k == 0 else 0))
                            wv = [wsp[:, c, part, 0:fn * P].rearrange("p (k c) -> p k c", k=fn) for part in range(2)]
                            feature_tile(dn, i, c, c, c, c, lambda part, _, k=k: wv[part][:, k, :], k, 1, asp, k == 0,
                                         k == fn - 1, k == fn - 1)
                rounds(pe, dn, dn_round)
            norm(5 * KT)

            for kq in range(4):
                pe.wait_ge(res_out, 2 * KT + 4 * kq + 4)
                for m in range(2):
                    for k in range(4 * kq, 4 * kq + 4):
                        mm = pe.transpose(ps[:, 2 * kq + m, (k % 4) * P:(k % 4 + 1) * P],
                                          big_b[:, k, m * P:(m + 1) * P], ident[:, :])
                    mm.then_inc(fin_turned, 1)

        @block.scalar
        def _(act):
            for m in range(2):
                act.dma_start(a_tok[:, m, :], x_tok[:, m, :]).then_inc(x_in, 16)
            act.wait_ge(prow_zero, 1)
            rows = [(0, G_PRE_MIX, "g_pre_mix"), (0, G_POST_MIX, "g_post_mix"), (0, G_PRE_X, "g_pre_x"),
                    (0, G_POST_X, "g_post_x"), (0, G_MEM, "g_mem"), (0, G_PRE_FFN, "g_pre_ffn"),
                    (0, G_POST_FFN, "g_post_ffn"), (0, B_CONV, "b_conv_lru"), (1, 0, "w_conv_lru"),
                    (1, B_RG - P, "b_rg"), (1, B_IG - P, "b_ig"), (1, LAM - P, "lru_lambda"), (1, G_CKV - P, "g_ckv"),
                    (2, 0, "w_fconv"), (5, 0, "b_fconv")]
            for tile, at, name in rows:
                src = a[name]
                if name == "w_fconv":
                    for kk in range(3):
                        act.dma_start(PROW[0:2 * FT, tile + kk, :], src[0, kk].rearrange("(r c) -> r c", c=P)).then_inc(par_in, 16)
                    continue
                if name == "w_conv_lru":
                    src = src[0].rearrange("k (r c) -> (k r) c", c=P)
                elif name in ("b_rg", "b_ig"):
                    src = src[0]
                else:
                    src = src[0].rearrange("(r c) -> r c", c=P)
                n = src.shape[0]
                act.dma_start(PROW[at:at + n, tile, :], src).then_inc(par_in, 16)
            act.dma_start(pos_i[:, :], a["positions"].to_broadcast([P, T])).then_inc(pos_in, 16)
            act.dma_start(invf[:, :], a["inv_freq"]).then_inc(pos_in, 16)

            own = Tally(act, act_self)

            def root(n, out_, in_, scale=1.0):
                act.wait_ge(var_ready, n)
                act.activation(out_, in_, ACT.Sqrt, scale=scale).then_inc(root_ready, 1)

            def hi(ph, i, c):
                p0 = ph.p0 + c
                if isinstance(i, int) and ph.p(i, c) >= PIECES:
                    return
                if c >= SLOTS and c - SLOTS < ph.n:
                    act.wait_ge(gemm_step, ph.g(i, ph.used[c - SLOTS]))
                elif not isinstance(i, int) or ph.g(i, 0) > 0:
                    act.wait_ge(gemm_step, ph.g(i, 0))
                act.wait_ge(landed[p0 % SLOTS], ph.landed(i, c))
                n = piece_size(ph, c)
                act.activation(wsp[:, p0 % SLOTS, 0, 0:n], raw[:, p0 % SLOTS, 0:n], ACT.Copy).then_inc(hi_done, 1)

            def cross(ph, i, j, slot=None, bank=None):
                slot = j % 4 if slot is None else slot
                bank = j % 4 if bank is None else bank
                act.wait_ge(gemm_step, ph.g(i, ph.done[j]))
                if not isinstance(i, int) or ph.t(i, j) >= 3:
                    act.wait_ge(tile_out, ph.t(i, j) - 2)
                act.activation(cr[:, slot, :], ps[:, bank, T:2 * T], ACT.Copy).then_inc(cross_done, 1)

            def plain(ph, post=None, per=0):
                own_before = own.n

                def body(i):
                    own.n, own.off = own_before, i * per
                    for c in range(4):
                        hi(ph, i, c + LEAD)
                        if c % 2:
                            for e in range(2):
                                cross(ph, i, c - 1 + e)
                            if post:
                                post(i, c)
                rounds(act, ph, body)
                own.n, own.off = own_before + per * ph.trips, 0

            for m in range(2):
                if m == 0:
                    act.wait_ge(x_in, 32)
                act.activation(b_tok[:, m, :], a_tok[:, m, :], ACT.Square, accum_out=st[:, m:m + 1]).then_inc(x_sq, 1)
            root(1, st[:, 4:6], st[:, 2:4])
            for p in range(LEAD):
                hi(PH_A, 0, p)
            act.wait_ge(par_ready, 4)
            act.activation(st[:, 48:64], st[:, 32:48], ACT.Exp, scale=-1.0).then_inc(lam_exp, 1)
            for k in range(KT):
                act.wait_ge(x_turned, k - k % 2 + 2)
                act.activation(hsp[:, k, 0:T], ps[:, k // 2, (k % 2) * T:(k % 2 + 1) * T], ACT.Copy,
                               scale=par[:, G_PRE_MIX + k:G_PRE_MIX + k + 1]).then_inc(x_hi, 1)
            for c in range(8):
                hi(PH_A, 0, c + LEAD)
            for j in range(5):
                cross(PH_A, 0, j, slot=(j + 3) % 4, bank=j)
            for j in range(RT):
                act.wait_ge(tile_out, j + 1)
                act.activation(SQ[j], CKV[j], ACT.Square).then_inc(ckv_sq, 1)
            hi(PH_Q0, 0, 2)
            root(2, RS, RV)
            hi(PH_Q0, 0, 3)
            act.wait_ge(angle_ready, 2)
            act.activation(SIN, SIN, ACT.Sin).then_inc(table_ready, 1)
            act.activation(COS, COS, ACT.Sin).then_inc(table_ready, 1)
            for j in range(RT):
                act.wait_ge(ckv_norm, j + 1)
                act.activation(asp[:, j, 0:T], CKV[j], ACT.Copy,
                               scale=par[:, G_CKV + j:G_CKV + j + 1]).then_inc(ckv_hi, 1)
            hi(PH_Q0, 0, 4)
            hi(PH_Q0, 0, 5)
            for n, b in enumerate(Q_ORDER):
                cross(PH_Q0, 0, n, slot=n, bank=b)

            def ukv(i):
                for c in range(4):
                    hi(PH_UKV, i, c + LEAD)
                    for j in range(4):
                        cross(PH_UKV, i, 4 * c + j)
            rounds(act, PH_UKV, ukv)

            def attention(u, ph):
                if ph:
                    hi(ph, u, 2)
                    hi(ph, u, 3)
                act.wait_ge(neg_max, u + 1)
                for e in range(2):
                    for q in range(2):
                        n = 2 * e + q
                        blk = PR[e][:, P * q:P * q + P * (q + 1)]
                        act.activation(blk, blk, ACT.Exp, bias=st[:, 12 + n:13 + n],
                                       accum_out=st[:, 16 + n:17 + n]).then_inc(exps_done, 1)
                if ph:
                    hi(ph, u, 4)
                for e in range(2):
                    act.wait_ge(probs_turned, u * 2 + e + 1)
                    act.activation(PT[e], ps[:, 5 + 2 * e, 0:384], ACT.Copy).then_inc(probs_copied, 1)
                if ph:
                    hi(ph, u, 5)
                    for n, b in enumerate(Q_ORDER):
                        cross(ph, u, n, slot=n, bank=b)
                act.wait_ge(pv_done, u + 1)
                act.activation(asp[:, bass.ds(u * 2, 2), 0:T], ps[:, 6, :].rearrange("p (e t) -> p e t", e=2),
                               ACT.Copy).then_inc(o_hi, 1)
            rounds(act, PH_Q, lambda i: attention(i, PH_Q))
            attention(HEADS // 2 - 1, None)
            for m in range(2):
                act.dma_start(b_tok[:, m, :], mem_tok[:, m, :]).then_inc(mem_in, 16)
            for g, w in enumerate((w_rg, w_ig)):
                act.dma_start(GW[:, g, :, :], w[:, 0:2, :]).then_inc(gate_w_in, 16)

            def sig(i, c):
                for e in range(2):
                    act.wait_ge(tile_out, PH_GM.t(i, c + e))
                    m = big_a[:, bass.ds(i * 4 + c - 1 + e, 1), :].rearrange("p a t -> p (a t)")
                    act.activation(m, m, ACT.Sigmoid).then_inc(gate_done, 1)
            plain(PH_GM, sig)
            act.wait_ge(mem_in, 32)
            for m in range(2):
                act.activation(scr[:, 2048:4096], b_tok[:, m, :], ACT.Square, accum_out=st[:, m:m + 1]).then_inc(mem_sq, 1)
                act.wait_ge(mem_sq, m + 1)
            root(3, st[:, 4:6], st[:, 2:4])
            plain(PH_OM)

            def lru(i):
                ph = PH_LRU
                hi(ph, i, 2)
                hi(ph, i, 3)
                for e in range(2):
                    cross(ph, i, e)
                hi(ph, i, 4)
                for e in range(2):
                    act.wait_ge(gates_mm, i * 2 + e + 1)
                    for g, (buf, b) in enumerate(((RG, B_RG), (IG, B_IG))):
                        act.activation(buf[e], ps[:, 4 + e, g * T:(g + 1) * T], ACT.Sigmoid,
                                       bias=par[:, bass.ds(i * 2 + b + e, 1)]).then_inc(gates_act, 1)
                for e in range(2):
                    act.wait_ge(gates_act, i * 4 + 2 * e + 2)
                    act.activation(TH[e], RG[e], ACT.Tanh, scale=par[:, bass.ds(i * 2 + LAM + e, 1)]).then_inc(lru_t, 1)
                for e in range(2):
                    act.wait_ge(lru_t, i * 2 + e + 1)
                    act.activation(SQT[e], TH[e], ACT.Sqrt, scale=4.0).then_inc(lru_root, 1)
                if not isinstance(i, int):
                    for g, w in enumerate((w_rg, w_ig)):
                        act.dma_start(GW[:, g, :, :], w[:, bass.ds(i * 2 + 2, 2), :]).then_inc(gate_w_in, 16)
                hi(ph, i, 5)
                for e in range(2):
                    cross(ph, i, 2 + e)
                for e in range(2):
                    act.wait_ge(tile_out, ph.t(i, 2 + e) + 1)
                    act.activation(XR[e], YY[e], ACT.Square, scale=0.044715 ** 0.5).then_inc(y_sq, 1)
                for e in range(2):
                    act.wait_ge(y_poly, i * 2 + e + 1)
                    act.activation(XR[e], XR[e], ACT.Sigmoid, scale=GELU_C).then_inc(y_sig, 1)
                for e in range(2):
                    act.wait_ge(hrg, i * 2 + e + 1)
                    act.activation(asp[:, bass.ds(i * 2 + e, 1), 0:T].rearrange("p a t -> p (a t)"), RG[e],
                                   ACT.Copy).then_inc(hrg_hi, 1)
            rounds(act, PH_LRU, lru, last_apart=True)

            def o_lru(i, c):
                if c == 3:
                    for e in range(2):
                        act.wait_ge(tile_out, PH_OL.t(i, 2 + e) + 1)
                        act.activation(OL_G[e], OL_G[e], ACT.Sigmoid).then_inc(olg_sig, 1)
            plain(PH_OL, o_lru)

            act.wait_ge(gemm_step, PH_OL.g_end)
            act.wait_ge(merged_out, KT)
            for k in range(KT // 2):
                act.activation(hsp[:, 2 * k:2 * k + 2, 0:T], big_a[:, 2 * k:2 * k + 2, :], ACT.Copy).then_inc(m_hi, 1)

            def wo(i):
                for c in range(4):
                    hi(PH_WO, i, c + LEAD)
                    if isinstance(i, int) and c < 2:
                        for k in range(8 * c, 8 * c + 8):
                            act.wait_ge(mem_turned, k - k % 2 + 2)
                            act.activation(asp[:, k, 0:T], ps[:, 4 + (k // 2) % 4, (k % 2) * T:(k % 2 + 1) * T], ACT.Copy,
                                           scale=par[:, G_MEM + k:G_MEM + k + 1]).then_inc(mem_hi, 1)
                    if c % 2:
                        for e in range(2):
                            cross(PH_WO, i, c - 1 + e)
            wo(0)
            act.wait_ge(m_lo, KT // 2)
            act.dma_start(a_tok, x_tok).then_inc(x2_in, 16)
            with act.Fori(1, PH_WO.trips) as i:
                wo(i)

            def residual(k, g, base):
                act.wait_ge(res_out, base + k + 1)
                act.wait_ge(ysq_done, KT + 2 * base + max(k - 1, 0))
                act.activation(ACS[k % 2], big_b[:, k, :], ACT.Square).then_inc(res_sq, 1)
                act.activation(hsp[:, k, 0:T], big_b[:, k, :], ACT.Copy,
                               scale=par[:, g + k:g + k + 1]).then_inc(res_hi, 1)

            res_at = {(0, 1): (0, 2), (0, 2): (2, 5), (0, 3): (5, 8), (1, 0): (8, 11), (1, 1): (11, 14), (1, 2): (14, 16)}
            for n, ph in enumerate((PH_CK, PH_CV)):
                for c in range(4):
                    hi(ph, 0, c + LEAD)
                    if c % 2:
                        for e in range(2):
                            cross(ph, 0, c - 1 + e)
                    if (n, c) == (0, 0):
                        root(4, RS, RV)
                    for k in range(*res_at.get((n, c), (0, 0))):
                        residual(k, G_PRE_X, 0)
            root(5, RS, RV)
            plain(PH_CQ)
            for h in range(XH):
                act.wait_ge(neg_max, HEADS // 2 + h + 1)
                for q in range(2):
                    act.activation(XP[h % 2][:, q, :], ps[:, 4 + h % 2, q * T:(q + 1) * T], ACT.Exp,
                                   bias=xst(h, 1)[:, q:q + 1], scale=XSCALE, accum_out=xst(h, 2)[:, q:q + 1]).then_inc(exps_done, 1)
                act.wait_ge(probs_turned, HEADS + h + 1)
                act.activation(XPT[h % 2], ps[:, 6, :].rearrange("p (m t) -> p m t", m=2), ACT.Copy).then_inc(probs_copied, 1)
                act.wait_ge(pv_done, HEADS // 2 + h + 1)
                act.activation(asp[:, h, 0:T], ps[:, 7, 0:T], ACT.Copy).then_inc(o_hi, 1)
            for c in range(4):
                hi(PH_CO, 0, c + LEAD)
                for j in range(4):
                    cross(PH_CO, 0, 4 * c + j)
            root(6, RS, RV)
            for k in range(KT):
                residual(k, G_PRE_FFN, KT)

            for n, ((f0, fn), up, dn) in enumerate(zip(GROUPS, PH_UP, PH_DN)):
                def up_round(i, first=False):
                    def bias(v):
                        for e in range(2):
                            act.wait_ge(tile_out, up.t(i, 2 * v + e) + 1)
                            m = i * 2 + f0 + e + v * FT
                            act.activation(UC[2 * v + e], UR[2 * v + e], ACT.Identity, scale=col(W_F + 2 * P, m),
                                           bias=col(B_F, m)).then_inc(up_bias, 1)
                    hi(up, i, 2)
                    hi(up, i, 3)
                    if first:
                        root(7, RS, RV)
                    for e in range(2):
                        cross(up, i, e)
                    bias(0)
                    hi(up, i, 4)
                    for e in range(2):
                        act.wait_ge(up_conv, i * 4 + 2 * f0 + e + 1)
                        act.activation(UC[e], UC[e], ACT.Gelu_apprx_tanh).then_inc(gelu_done, 1)
                    hi(up, i, 5)
                    for e in range(2):
                        cross(up, i, 2 + e)
                    bias(1)
                    for e in range(2):
                        act.wait_ge(hid_out, i * 2 + f0 + e + 1)
                        act.activation(asp[:, bass.ds(i * 2 + e, 1), 0:T].rearrange("p a t -> p (a t)"), HID[e],
                                       ACT.Copy).then_inc(hid_hi, 1)
                if n == 0:
                    up_round(0, True)
                    with act.Fori(1, up.trips) as i:
                        up_round(i)
                else:
                    rounds(act, up, up_round)

                def dn_round(i):
                    for c in range(4):
                        hi(dn, i, c + LEAD)
                        cross(dn, i, c)
                rounds(act, dn, dn_round, last_apart=(n == len(GROUPS) - 1))
            root(8, RS, RV)
            for kq in range(4):
                for m in range(2):
                    act.wait_ge(fin_turned, 2 * kq + m + 1)
                    act.activation(out_sb[:, m, kq * 512:(kq + 1) * 512], ps[:, 2 * kq + m, :], ACT.Copy).then_inc(fin_copied, 1)

        @block.vector
        def _(dve):
            own = Tally(dve, dve_self)

            def lo(ph, i, c):
                p0 = ph.p0 + c
                if isinstance(i, int) and ph.p(i, c) >= PIECES:
                    return
                dve.wait_ge(hi_done, ph.p(i, c) + 1)
                n, slot = piece_size(ph, c), p0 % SLOTS
                dve.tensor_tensor(wsp[:, slot, 1, 0:n], raw[:, slot, 0:n], wsp[:, slot, 0, 0:n].bitcast(F32),
                                  ALU.subtract).then_inc(lo_done, 1)

            def add(ph, i, j, dst, slot=None, bank=None):
                slot = j % 4 if slot is None else slot
                bank = j % 4 if bank is None else bank
                dve.wait_ge(cross_done, ph.t(i, j) + 1)
                return dve.tensor_tensor(dst, ps[:, bank, 0:T], cr[:, slot, :], ALU.add)

            def tile_at(buf, m):
                return buf[:, bass.ds(m, 1), :].rearrange("p a t -> p (a t)")

            def small_rms(n, src_sem, count, var, rt, r):
                dve.wait_ge(src_sem, count)
                dve.tensor_scalar(st[:, 2:4], st[:, 0:2], 1.0 / D, EPS, ALU.mult, ALU.add).then_inc(var_ready, 1)
                dve.wait_ge(root_ready, n)
                newton(st[:, 2:4], st[:, 4:6], st[:, 6:8], st[:, 26:28])

            def newton(v, root_, r0, r):
                own.link(dve.reciprocal(r0, root_))
                own.link(dve.tensor_tensor(r, r0, r0, ALU.mult))
                own.link(dve.tensor_tensor(r, r, v, ALU.mult))
                own.link(dve.tensor_scalar(r, r, -0.5, 1.5, ALU.mult, ALU.add))
                ins = dve.tensor_tensor(r, r, r0, ALU.mult)
                ins.then_inc(rms_ready, 1)
                rms_n[0] += 1
                dve.wait_ge(rms_ready, rms_n[0])
            rms_n = [0]

            def rms(n, sum_sem, count, bank, width):
                dve.wait_ge(sum_sem, count)
                dve.tensor_scalar(RV, ps[:, bank, 0:T], 1.0 / width, EPS, ALU.mult, ALU.add).then_inc(var_ready, 1)
                dve.wait_ge(root_ready, n)
                newton(RV, RS, RT0, RR)

            dve.wait_ge(par_turned, 6)
            dve.tensor_copy(par[:, 0:4 * P], ps[:, 4, :]).then_inc(par_ready, 1)
            dve.tensor_copy(par[:, 4 * P:6 * P], ps[:, 5, 0:2 * P]).then_inc(par_ready, 1)
            dve.wait_ge(par_ready, 2)
            lam = par[:, LAM:LAM + KT]
            dve.scalar_tensor_tensor(out=st[:, 32:48], in0=lam, scalar=-1.0, in1=lam, op0=ALU.mult, op1=ALU.max).then_inc(par_ready, 1)
            dve.tensor_scalar(lam, lam, -4.0, 0.0, ALU.mult, ALU.max).then_inc(par_ready, 1)
            small_rms(1, x_sq, 2, 2, 4, 6)
            for m in range(2):
                dve.tensor_scalar(a_tok[:, m, :], a_tok[:, m, :], st[:, 26 + m:27 + m], None, ALU.mult).then_inc(x_scaled, 1)
            for c in range(LEAD):
                lo(PH_A, 0, c)
            for k in range(KT):
                dve.wait_ge(x_hi, k - k % 2 + 2)
                dve.scalar_tensor_tensor(out=hsp[:, k, T:2 * T], in0=ps[:, k // 2, (k % 2) * T:(k % 2 + 1) * T],
                                         scalar=par[:, G_PRE_MIX + k:G_PRE_MIX + k + 1], in1=hsp[:, k, 0:T].bitcast(F32),
                                         op0=ALU.mult, op1=ALU.subtract).then_inc(x_lo, 1)
            for c in range(8):
                lo(PH_A, 0, c + LEAD)
                if c == 1:
                    e_, s_, s2, p_ = st[:, 48:64], st[:, 32:48], st[:, 64:80], st[:, 80:96]
                    dve.wait_ge(lam_exp, 1)
                    own.link(dve.tensor_scalar(s_, e_, 2.0, None, ALU.add))
                    own.link(dve.reciprocal(s_, s_))
                    own.link(dve.tensor_tensor(s_, s_, e_, ALU.mult))
                    own.link(dve.tensor_tensor(s2, s_, s_, ALU.mult))
                    own.link(dve.tensor_scalar(p_, s2, 1.0 / 17, None, ALU.mult))
                    for n in (15, 13, 11, 9, 7, 5, 3):
                        own.link(dve.scalar_tensor_tensor(out=p_, in0=p_, scalar=1.0 / n, in1=s2, op0=ALU.add, op1=ALU.mult))
                    own.link(dve.scalar_tensor_tensor(out=p_, in0=p_, scalar=1.0, in1=s_, op0=ALU.add, op1=ALU.mult))
                    own.link(dve.scalar_tensor_tensor(out=lam, in0=p_, scalar=8.0, in1=lam, op0=ALU.mult, op1=ALU.add))
                if c == 3:
                    dve.wait_ge(pos_in, 32)
                    own.link(dve.tensor_copy(COS, pos_i[:, :]))
                    own.link(dve.tensor_scalar(COS, COS, invf[:, 0:1], None, ALU.mult))
                    own.link(dve.tensor_scalar(SIN, COS, 1.0 / (2 * PI), MAGIC, ALU.mult, ALU.add))
                    own.link(dve.tensor_scalar(SIN, SIN, -MAGIC, None, ALU.add))
                    for part in TWO_PI:
                        own.link(dve.scalar_tensor_tensor(out=COS, in0=SIN, scalar=-part, in1=COS, op0=ALU.mult, op1=ALU.add))
                    own.link(dve.tensor_scalar(SIN, COS, 3.1415925, -3.1415925, ALU.min, ALU.max))
                    own.link(dve.scalar_tensor_tensor(out=COS, in0=SIN, scalar=-1.0, in1=SIN, op0=ALU.mult, op1=ALU.max))
                    dve.tensor_scalar(COS, COS, -1.0, PI / 2, ALU.mult, ALU.add).then_inc(angle_ready, 2)
            for j in range(RT):
                add(PH_A, 0, j, CKV[j], slot=(j + 3) % 4, bank=j).then_inc(tile_out, 1)
            dve.wait_ge(cross_done, 5)
            for to in (0, 64):
                ins = dve.tensor_tensor(KRAW[to:to + 64, :], ps[64:P, 4, 0:T], cr[64:P, 3, :], ALU.add)
            ins.then_inc(tile_out, 1)
            lo(PH_Q0, 0, 2)
            rms(2, ckv_sum, 1, 5, RANK)
            for j in range(RT):
                dve.tensor_tensor(CKV[j], CKV[j], RR, ALU.mult).then_inc(ckv_norm, 1)
            lo(PH_Q0, 0, 3)

            def rotate(n, dst, src):
                dve.wait_ge(rot_done, n)
                own.link(dve.tensor_tensor(ROTT, ps[:, 6, 0:T], SIN, ALU.mult))
                own.link(dve.tensor_tensor(dst, src, COS, ALU.mult))
                dve.tensor_tensor(dst, dst, ROTT, ALU.add).then_inc(roped, 1)
            dve.wait_ge(table_ready, 2)
            dve.wait_ge(tile_out, 5)
            rotate(1, KR, KRAW)
            for j in range(RT):
                dve.wait_ge(ckv_hi, j + 1)
                dve.scalar_tensor_tensor(out=asp[:, j, T:2 * T], in0=CKV[j], scalar=par[:, G_CKV + j:G_CKV + j + 1],
                                         in1=asp[:, j, 0:T].bitcast(F32), op0=ALU.mult, op1=ALU.subtract).then_inc(ckv_lo, 1)
            lo(PH_Q0, 0, 4)
            lo(PH_Q0, 0, 5)

            def q_out(ph, i):
                low, high = slice(0, 64), slice(64, P)
                moves = {1: [(low, QRAW, low), (high, QN[1], low)],
                         2: [(low, QN[1], high), (high, QRAW, high)]}
                for n, b in enumerate(Q_ORDER):
                    dve.wait_ge(cross_done, ph.t(i, n) + 1)
                    if b == 0:
                        ins = dve.tensor_tensor(QN[0], ps[:, b, 0:T], cr[:, n, :], ALU.add)
                    else:
                        for src, dst, to in moves[b]:
                            ins = dve.tensor_tensor(dst[to, :], ps[src, b, 0:T], cr[src, n, :], ALU.add)
                    ins.then_inc(tile_out, 1)
            q_out(PH_Q0, 0)

            def ukv(i):
                for c in range(4):
                    lo(PH_UKV, i, c + LEAD)
                    for j in range(2):
                        add(PH_UKV, i, 4 * c + j, tile_at(big_a, i * 8 + 2 * c + j)).then_inc(tile_out, 1)
                    for m in range(2):
                        add(PH_UKV, i, 4 * c + 2 + m, b_tok[:, m, bass.ds(i * 1024 + c * T, T)]).then_inc(tile_out, 1)
            rounds(dve, PH_UKV, ukv)

            def attention(u, ph, per=0):
                own.off = u * per if ph else 0
                dve.wait_ge(tile_out, PH_Q.t(u, 0) - 1)
                rotate(u + 2, QROPE, QRAW)
                if ph:
                    lo(ph, u, 2)
                    lo(ph, u, 3)
                for e in range(2):
                    dve.wait_ge(scores_done, u * 2 + e + 1)
                    own.link(dve.scalar_tensor_tensor(out=PR[e], in0=ps[:, 3 + e, 0:384], scalar=SCALE, in1=mask[:, :],
                                                      op0=ALU.mult, op1=ALU.add))
                    own.mark(dve.tensor_reduce(st[:, 8 + 2 * e:9 + 2 * e], PR[e][:, 0:P], AX, ALU.max))
                    own.link(dve.tensor_reduce(st[:, 9 + 2 * e:10 + 2 * e], PR[e][:, P:3 * P], AX, ALU.max))
                dve.tensor_scalar(st[:, 12:16], st[:, 8:12], -1.0, None, ALU.mult).then_inc(neg_max, 1)
                dve.wait_ge(exps_done, u * 4 + 4)
                dve.reciprocal(st[:, 20:24], st[:, 16:20]).then_inc(sums_inv, 1)
                if ph:
                    lo(ph, u, 4)
                    lo(ph, u, 5)
                    q_out(ph, u)
                dve.wait_ge(o_hi, u + 1)
                dve.tensor_tensor(asp[:, bass.ds(u * 2, 2), T:2 * T], ps[:, 6, :].rearrange("p (e t) -> p e t", e=2),
                                  asp[:, bass.ds(u * 2, 2), 0:T].bitcast(F32), ALU.subtract).then_inc(o_lo, 1)
            n0 = own.n
            dve.wait_ge(mask_made, 2)
            rounds(dve, PH_Q, lambda i: attention(i, PH_Q, 8))
            assert own.n == n0 + 8
            own.n, own.off = n0 + 8 * PH_Q.trips, 0
            attention(HEADS // 2 - 1, None)

            def gm(i):
                for c in range(4):
                    lo(PH_GM, i, c + LEAD)
                    if c % 2:
                        for e in range(2):
                            add(PH_GM, i, c - 1 + e, tile_at(big_a, i * 4 + c - 1 + e)).then_inc(tile_out, 1)
            rounds(dve, PH_GM, gm)
            small_rms(3, mem_sq, 2, 2, 4, 6)
            for m in range(2):
                dve.tensor_scalar(b_tok[:, m, :], b_tok[:, m, :], st[:, 26 + m:27 + m], None, ALU.mult).then_inc(mem_scaled, 1)
            dve.wait_ge(gate_done, KT)
            n0 = own.n

            def om(i):
                own.n, own.off = n0, i * 4
                for c in range(4):
                    lo(PH_OM, i, c + LEAD)
                    if c % 2:
                        for e in range(2):
                            own.mark(add(PH_OM, i, c - 1 + e, cr[:, c - 1 + e, :]))
                        for e in range(2):
                            dve.wait_ge(dve_self, own.now() - 1 + e)
                            g = tile_at(big_a, i * 4 + c - 1 + e)
                            dve.tensor_tensor(g, g, cr[:, c - 1 + e, :], ALU.mult).then_inc(tile_out, 1)
            rounds(dve, PH_OM, om)
            own.n, own.off = n0 + 4 * PH_OM.trips, 0
            n0 = own.n

            def lru(i):
                ph = PH_LRU
                own.n, own.off = n0, i * 8
                lo(ph, i, 2)
                lo(ph, i, 3)
                dve.wait_ge(hrg, i * 2)
                for e in range(2):
                    add(ph, i, e, XR[e]).then_inc(tile_out, 1)
                for e in range(2):
                    dve.wait_ge(tile_out, ph.t(i, e) + 1)
                    own.mark(dve.tensor_scalar(XC[e], XR[e], par[:, bass.ds(i * 2 + W_CONV + 48 + e, 1)],
                                               par[:, bass.ds(i * 2 + B_CONV + e, 1)], ALU.mult, ALU.add))
                for d in (1, 2, 3):
                    for e in range(2):
                        dve.wait_ge(dve_self, own.now() - 1 + (e if d == 3 else 0))
                        ins = dve.scalar_tensor_tensor(out=XC[e][:, d:T], in0=XR[e][:, 0:T - d],
                                                       scalar=par[:, bass.ds(i * 2 + W_CONV + 16 * (3 - d) + e, 1)],
                                                       in1=XC[e][:, d:T], op0=ALU.mult, op1=ALU.add)
                        if d == 3:
                            ins.then_inc(conv_done, 1)
                        else:
                            own.mark(ins)
                lo(ph, i, 4)
                for e in range(2):
                    dve.wait_ge(lru_t, i * 2 + e + 1)
                    own.mark(dve.tensor_scalar(RC[e], TH[e], 1.0, None, ALU.add))
                for e in range(2):
                    dve.wait_ge(dve_self, own.now() - 1 + e)
                    dve.reciprocal(RC[e], RC[e]).then_inc(lru_rc, 1)
                lo(ph, i, 5)
                for e in range(2):
                    add(ph, i, 2 + e, YY[e]).then_inc(tile_out, 1)
                for e in range(2):
                    dve.wait_ge(lru_a, i * 2 + e + 1)
                    dve.tensor_tensor_scan(TH[e], RC[e], SQT[e], 0.0, ALU.mult, ALU.add).then_inc(lru_scan, 1)
                for e in range(2):
                    dve.wait_ge(hrg_hi, i * 2 + e + 1)
                    m = asp[:, bass.ds(i * 2 + e, 1), :].rearrange("p a t -> p (a t)")
                    dve.tensor_tensor(m[:, T:2 * T], RG[e], m[:, 0:T].bitcast(F32), ALU.subtract).then_inc(hrg_lo, 1)
                assert own.n == n0 + 8
            rounds(dve, PH_LRU, lru)
            own.n, own.off = n0 + 8 * PH_LRU.trips, 0

            def o_lru(i):
                for c in range(4):
                    lo(PH_OL, i, c + LEAD)
                    if c % 2:
                        dve.wait_ge(merged_out, i * 2)
                        for e in range(2):
                            add(PH_OL, i, c - 1 + e, (OL_O if c == 1 else OL_G)[e]).then_inc(tile_out, 1)
            rounds(dve, PH_OL, o_lru)

            for k in range(KT // 2):
                dve.wait_ge(m_hi, k + 1)
                dve.tensor_tensor(hsp[:, 2 * k:2 * k + 2, T:2 * T], big_a[:, 2 * k:2 * k + 2, :],
                                  hsp[:, 2 * k:2 * k + 2, 0:T].bitcast(F32), ALU.subtract).then_inc(m_lo, 1)

            def wo(i):
                for c in range(4):
                    lo(PH_WO, i, c + LEAD)
                    if isinstance(i, int) and c < 2:
                        for k in range(8 * c, 8 * c + 8):
                            dve.wait_ge(mem_hi, k - k % 2 + 2)
                            dve.scalar_tensor_tensor(out=asp[:, k, T:2 * T], in0=ps[:, 4 + (k // 2) % 4, (k % 2) * T:(k % 2 + 1) * T],
                                                     scalar=par[:, G_MEM + k:G_MEM + k + 1], in1=asp[:, k, 0:T].bitcast(F32),
                                                     op0=ALU.mult, op1=ALU.subtract).then_inc(mem_lo, 1)
                    if c % 2:
                        for e in range(2):
                            add(PH_WO, i, c - 1 + e, tile_at(big_b, i * 4 + c - 1 + e)).then_inc(tile_out, 1)
            wo(0)
            with dve.Fori(1, PH_WO.trips) as i:
                wo(i)

            def residual(k, g_post, g_pre, base, xt):
                dve.wait_ge(y_scaled, base + k + 1)
                b = big_b[:, k, :]
                if xt:
                    dve.wait_ge(xt_turned, k + 1)
                    dve.scalar_tensor_tensor(out=b, in0=b, scalar=par[:, g_post + k:g_post + k + 1],
                                             in1=ps[:, 5 + k % 3, 0:T], op0=ALU.mult, op1=ALU.add).then_inc(res_out, 1)
                else:
                    dve.scalar_tensor_tensor(out=b, in0=big_a[:, k, :], scalar=par[:, g_post + k:g_post + k + 1],
                                             in1=b, op0=ALU.mult, op1=ALU.add).then_inc(res_out, 1)
                if g_pre is not None:
                    dve.wait_ge(res_hi, base + k + 1)
                    dve.scalar_tensor_tensor(out=hsp[:, k, T:2 * T], in0=b, scalar=par[:, g_pre + k:g_pre + k + 1],
                                             in1=hsp[:, k, 0:T].bitcast(F32), op0=ALU.mult, op1=ALU.subtract).then_inc(res_lo, 1)

            res_at = {(0, 1): (0, 2), (0, 2): (2, 5), (0, 3): (5, 8), (1, 0): (8, 11), (1, 1): (11, 14), (1, 2): (14, 16)}
            for n, ph in enumerate((PH_CK, PH_CV)):
                for c in range(4):
                    lo(ph, 0, c + LEAD)
                    if c % 2:
                        for e in range(2):
                            j = c - 1 + e
                            dst = CKT[j] if n == 0 else CVT[:, e, (c // 2) * T:(c // 2 + 1) * T]
                            add(ph, 0, j, dst).then_inc(tile_out, 1)
                    if (n, c) == (0, 0):
                        rms(4, norm_sum, 1, 4, D)
                    for k in range(*res_at.get((n, c), (0, 0))):
                        residual(k, G_POST_MIX, G_PRE_X, 0, True)
            rms(5, norm_sum, 2, 4, D)
            for c in range(4):
                lo(PH_CQ, 0, c + LEAD)
                if c % 2:
                    for e in range(2):
                        j = c - 1 + e
                        own.link(add(PH_CQ, 0, j, cr[:, j, :]))
                        dve.tensor_tensor(CQ[j], cr[:, j, :], RR, ALU.mult).then_inc(tile_out, 1)
            for h in range(XH):
                dve.wait_ge(scores_done, HEADS + h + 1)
                own.link(dve.tensor_reduce(xst(h, 0), ps[:, 4 + h % 2, :].rearrange("p (q t) -> p q t", q=2), AX, ALU.max))
                dve.tensor_scalar(xst(h, 1), xst(h, 0), -XSCALE, None, ALU.mult).then_inc(neg_max, 1)
                dve.wait_ge(exps_done, 2 * HEADS + 2 * h + 2)
                dve.reciprocal(xst(h, 3), xst(h, 2)).then_inc(sums_inv, 1)
                dve.wait_ge(o_hi, HEADS // 2 + h + 1)
                dve.tensor_tensor(asp[:, h, T:2 * T], ps[:, 7, 0:T], asp[:, h, 0:T].bitcast(F32), ALU.subtract).then_inc(o_lo, 1)
            for c in range(4):
                lo(PH_CO, 0, c + LEAD)
                for j in range(4):
                    add(PH_CO, 0, 4 * c + j, big_a[:, 4 * c + j, :]).then_inc(tile_out, 1)
            rms(6, norm_sum, 3, 4, D)
            for k in range(KT):
                residual(k, G_POST_X, G_PRE_FFN, KT, False)

            for n, ((f0, fn), up, dn) in enumerate(zip(GROUPS, PH_UP, PH_DN)):
                n0 = own.n

                def up_round(i, first=False):
                    def unit(v):
                        for e in range(2):
                            own.mark(add(up, i, 2 * v + e, cr[:, 2 * v + e, :]))
                        for e in range(2):
                            dve.wait_ge(dve_self, own.now() - 1 + e)
                            dve.tensor_tensor(UR[2 * v + e], cr[:, 2 * v + e, :], RR, ALU.mult).then_inc(tile_out, 1)
                        for e in range(2):
                            m = i * 2 + f0 + e + v * FT
                            dve.wait_ge(up_bias, i * 4 + 2 * f0 + 2 * v + e + 1)
                            buf, src = UC[2 * v + e], UR[2 * v + e]
                            own.mark(dve.scalar_tensor_tensor(out=buf[:, 1:T], in0=src[:, 0:T - 1], scalar=col(W_F + P, m),
                                                              in1=buf[:, 1:T], op0=ALU.mult, op1=ALU.add))
                        for e in range(2):
                            m = i * 2 + f0 + e + v * FT
                            dve.wait_ge(dve_self, own.now() - 1 + e)
                            buf, src = UC[2 * v + e], UR[2 * v + e]
                            dve.scalar_tensor_tensor(out=buf[:, 2:T], in0=src[:, 0:T - 2], scalar=col(W_F, m),
                                                     in1=buf[:, 2:T], op0=ALU.mult, op1=ALU.add).then_inc(up_conv, 1)
                    if first:
                        lo(up, i, 2)
                        lo(up, i, 3)
                        rms(7, norm_sum, 4, 4, D)
                        base[0] = own.n
                    own.n, own.off = base[0], i * 8
                    if not first:
                        lo(up, i, 2)
                        lo(up, i, 3)
                    unit(0)
                    lo(up, i, 4)
                    lo(up, i, 5)
                    unit(1)
                    for e in range(2):
                        dve.wait_ge(hid_hi, i * 2 + f0 + e + 1)
                        m = asp[:, bass.ds(i * 2 + e, 1), :].rearrange("p a t -> p (a t)")
                        dve.tensor_tensor(m[:, T:2 * T], HID[e], m[:, 0:T].bitcast(F32), ALU.subtract).then_inc(hid_lo, 1)
                    assert own.n == base[0] + 8
                base = [own.n]
                if n == 0:
                    up_round(0, True)
                    with dve.Fori(1, up.trips) as i:
                        up_round(i)
                else:
                    rounds(dve, up, up_round)
                own.n, own.off = base[0] + 8 * up.trips, 0
                n0d = own.n

                def dn_round(i):
                    own.n, own.off = n0d, i * 4
                    for c in range(4):
                        lo(dn, i, c + LEAD)
                        y = tile_at(big_a, i * 4 + c)
                        if n == 0:
                            add(dn, i, c, y).then_inc(tile_out, 1)
                        else:
                            own.link(add(dn, i, c, cr[:, c, :]))
                            dve.tensor_tensor(y, y, cr[:, c, :], ALU.add).then_inc(tile_out, 1)
                rounds(dve, dn, dn_round, last_apart=(n == len(GROUPS) - 1))
                if n:
                    own.n = n0d + 4 * dn.trips
                own.off = 0
            rms(8, norm_sum, 5, 4, D)
            for k in range(KT):
                residual(k, G_POST_FFN, None, 2 * KT, False)

        @block.gpsimd
        def _(pool):
            own = Tally(pool, pool_self)
            pool.memset(scr[:, 0:6 * P], 0.0).then_inc(prow_zero, 1)
            own.mark(pool.memset(ident[:, :], 0.0))
            own.mark(pool.memset(rotm[:, :], 0.0))
            own.link(pool.memset(mask[:, :], 0.0))
            pool.memset(ones[:, :], 1.0).then_inc(consts_made, 1)
            pool.affine_select(out=ident[:, :], in_=ident[:, :], compare_op=ALU.not_equal, fill=1.0, base=0,
                               pattern=[[-1, P]], channel_multiplier=1).then_inc(consts_made, 1)
            rv = rotm[:, :].rearrange("p (g h j) -> p g h j", g=2, h=2)
            for h, fill in ((0, -1.0), (1, 1.0)):
                ins = pool.affine_select(out=rv[:, :, h, :], in_=rv[:, :, h, :], compare_op=ALU.not_equal, fill=fill,
                                         base=-32 if h == 0 else 0, pattern=[[-64, 2], [-1, 32]], channel_multiplier=1)
                ins.then_inc(consts_made, 1)
            for q in range(2):
                blk = mask[:, 2 * q * P:(2 * q + 1) * P]
                ins = pool.affine_select(out=blk, in_=blk, compare_op=ALU.is_ge, fill=NEG, base=0, pattern=[[-1, P]],
                                         channel_multiplier=1)
                ins.then_inc(mask_made, 1)

            def attention(u):
                if isinstance(u, int):
                    pool.wait_ge(tile_out, PH_UKV.t_end)
                pool.wait_ge(pv_done, u)
                pool.tensor_copy(cur[:, :].rearrange("p (e t) -> p e t", e=2), big_a[:, bass.ds(u * 2, 2), :]).then_inc(kv_cur, 1)
                pool.tensor_copy(scr[:, 768:1280].rearrange("p (m d) -> p m d", m=2), b_tok[:, :, bass.ds(u * T, T)]).then_inc(kv_cur, 1)
                pool.wait_ge(sums_inv, u + 1)
                for e in range(2):
                    for q in range(2):
                        n = 2 * e + q
                        blk = PR[e][:, P * q:P * q + P * (q + 1)]
                        inv = st[:, 20 + n:21 + n].to_broadcast([P, P * (q + 1)])
                        pool.tensor_tensor(blk, blk, inv, ALU.mult).then_inc(probs_ready, 1)
            pool.wait_ge(tile_out, PH_UKV.t_end)
            with pool.Fori(0, HEADS // 2) as u:
                attention(u)

            n0 = own.n

            def lru(i):
                own.n, own.off = n0, i * 10
                for e in range(2):
                    pool.wait_ge(gates_act, i * 4 + 2 * e + 2)
                    own.mark(pool.tensor_tensor(IG[e], IG[e], XC[e], ALU.mult))
                    pool.wait_ge(lru_root, i * 2 + e + 1)
                    pool.wait_ge(lru_rc, i * 2 + e + 1)
                    own.mark(pool.tensor_tensor(SQT[e], SQT[e], RC[e], ALU.mult))
                    own.link(pool.tensor_scalar(RC[e], RC[e], 2.0, -1.0, ALU.mult, ALU.add))
                    pool.tensor_tensor(SQT[e], SQT[e], IG[e], ALU.mult).then_inc(lru_a, 1)
                for e in range(2):
                    pool.wait_ge(y_sq, i * 2 + e + 1)
                    own.link(pool.tensor_tensor(XR[e], XR[e], YY[e], ALU.mult))
                    pool.tensor_tensor(XR[e], XR[e], YY[e], ALU.add).then_inc(y_poly, 1)
                for e in range(2):
                    pool.wait_ge(y_sig, i * 2 + e + 1)
                    own.link(pool.tensor_tensor(XR[e], XR[e], YY[e], ALU.mult))
                    pool.wait_ge(lru_scan, i * 2 + e + 1)
                    pool.tensor_tensor(RG[e], XR[e], TH[e], ALU.mult).then_inc(hrg, 1)
                assert own.n == n0 + 10
            rounds(pool, PH_LRU, lru)
            own.n, own.off = n0 + 10 * PH_LRU.trips, 0
            n1 = own.n

            def o_lru(i):
                own.n, own.off = n1, i * 2
                for e in range(2):
                    pool.wait_ge(olg_sig, i * 2 + e + 1)
                    own.link(pool.tensor_tensor(OL_O[e], OL_O[e], OL_G[e], ALU.mult))
                    g = big_a[:, bass.ds(i * 2 + e, 1), :].rearrange("p a t -> p (a t)")
                    pool.tensor_tensor(g, g, OL_O[e], ALU.add).then_inc(merged_out, 1)
            rounds(pool, PH_OL, o_lru)
            own.n, own.off = n1 + 2 * PH_OL.trips, 0

            def add_square(tile_done, y, count, e):
                pool.wait_ge(tile_out, tile_done + 1)
                own.link(pool.tensor_tensor(ACS[e], y, y, ALU.mult))
                if not isinstance(count, int) or count:
                    pool.wait_ge(ysq_done, count)
                pool.tensor_tensor(ACC, ACC, ACS[e], ALU.add).then_inc(ysq_done, 1)

            own.link(pool.memset(ACC, 0.0))
            n2 = own.n

            def wo(i):
                own.n, own.off = n2, i * 4
                for j in range(4):
                    y = big_b[:, bass.ds(i * 4 + j, 1), :].rearrange("p a t -> p (a t)")
                    add_square(PH_WO.t(i, j), y, i * 4 + j, j % 2)
            rounds(pool, PH_WO, wo)
            own.n, own.off = n2 + 4 * PH_WO.trips, 0

            def scale_tiles(buf, n_rms, base, squares):
                if squares:
                    pool.wait_ge(norm_sum, 1 + base // 8)
                    own.link(pool.memset(ACC, 0.0))
                pool.wait_ge(rms_ready, n_rms)
                for k in range(KT + 1):
                    if k < KT:
                        pool.tensor_tensor(buf[:, k, :], buf[:, k, :], RR, ALU.mult).then_inc(y_scaled, 1)
                    if k and squares:
                        pool.wait_ge(res_sq, base + k)
                        pool.wait_ge(ysq_done, KT + 2 * base + k - 1)
                        pool.tensor_tensor(ACC, ACC, ACS[(k - 1) % 2], ALU.add).then_inc(ysq_done, 1)
            scale_tiles(big_b, 4, 0, True)

            for h in range(XH):
                pool.wait_ge(sums_inv, HEADS // 2 + h + 1)
                for q in range(2):
                    blk = XP[h % 2][:, q, :]
                    pool.tensor_scalar(blk, blk, xst(h, 3)[:, q:q + 1], None, ALU.mult).then_inc(probs_ready, 1)
            pool.wait_ge(norm_sum, 2)
            own.link(pool.memset(ACC, 0.0))
            for j in range(KT):
                add_square(PH_CO.t(0, j), big_a[:, j, :], 2 * KT + j, j % 2)
            scale_tiles(big_a, 6, KT, True)

            for (f0, fn), up in zip(GROUPS, PH_UP):
                def up_round(i):
                    for e in range(2):
                        done = i * 2 + f0 + e
                        pool.wait_ge(gelu_done, done + 1)
                        pool.wait_ge(up_conv, i * 4 + 2 * f0 + 2 + e + 1)
                        if not isinstance(i, int) or f0:
                            pool.wait_ge(hid_lo, i * 2 + f0)
                        pool.tensor_tensor(HID[e], UC[e], UC[2 + e], ALU.mult).then_inc(hid_out, 1)
                rounds(pool, up, up_round)
            own.link(pool.memset(ACC, 0.0))
            n3, dn = own.n, PH_DN[-1]

            def dn_round(i):
                own.n, own.off = n3, i * 4
                for j in range(4):
                    y = big_a[:, bass.ds(i * 4 + j, 1), :].rearrange("p a t -> p (a t)")
                    add_square(dn.t(i, j), y, i * 4 + 4 * KT + j, j % 2)
            rounds(pool, dn, dn_round)
            own.n, own.off = n3 + 4 * dn.trips, 0
            scale_tiles(big_a, 8, 2 * KT, False)


NAMES = ["x", "mem", "positions", "g_pre_mix", "g_post_mix", "w_in", "g_ckv", "w_ukv", "w_o_mla", "w_conv_lru",
         "b_conv_lru", "w_rg", "b_rg", "w_ig", "b_ig", "lru_lambda", "w_o_lru", "w_out", "g_pre_x", "g_post_x",
         "g_mem", "w_cq", "w_ck", "w_cv", "w_co", "g_pre_ffn", "g_post_ffn", "w_up", "w_fconv", "b_fconv", "w_down"]


def kernel(**inputs):
    import numpy as np
    import concourse.bacc as bacc
    from concourse.bass_utils import run_bass_kernel_spmd

    nc = bacc.Bacc("TRN2", target_bir_lowering=False, num_devices=1, dynamic_dma_scratch_size=1024)
    arrays = {name: np.ascontiguousarray(inputs[name]) for name in NAMES}
    freq = np.float32(10000.0) ** (-np.arange(0, ROPE, 2, dtype=np.float32) / np.float32(ROPE))
    arrays["inv_freq"] = np.tile(freq.astype(np.float32), 4).reshape(P, 1)
    aps = {name: nc.dram_tensor(f"in_{name}", v.shape, mybir.dt.from_np(v.dtype), kind="ExternalInput").ap()
           for name, v in arrays.items()}
    out = nc.dram_tensor("out", (1, T, D), F32, kind="ExternalOutput").ap()
    build(nc, aps, out)
    r = run_bass_kernel_spmd(nc, [{f"in_{name}": v for name, v in arrays.items()}], core_ids=[0])
    return r.results[0]["out"]
```

```python
from contextlib import ExitStack

import concourse.bass as bass
from concourse import mybir

F32 = mybir.dt.float32
F32R = mybir.dt.float32r
I32 = mybir.dt.int32
ALU = mybir.AluOpType
ACT = mybir.ActivationFunctionType
AX = mybir.AxisListType.X

P = 128
D = 2048
T = 256
KT = D // P
HEADS, NOPE, ROPE = 16, 128, 64
QH = NOPE + ROPE
RANK = 512
RT = RANK // P
XH = 4
DFF = 5632
FT = DFF // P
GROUPS = [(0, 16), (16, 16), (32, 12)]
EPS = 1e-6
SLOTS = 4
LEAD = 2
OFF_CKV = HEADS * QH
OFF_LX = OFF_CKV + RANK + ROPE
OFF_LY = OFF_LX + D
OFF_GM = OFF_LY + D
OFF_GL = OFF_GM + D
RES_AT = {(0, 1): (0, 2), (0, 2): (2, 5), (0, 3): (5, 8), (1, 0): (8, 11), (1, 1): (11, 14), (1, 2): (14, 16)}
TWO_PI = (6.28125, 0.0019350051879882812, 3.019916050561733e-07)
MAGIC = 12582912.0
PI = 3.141592653589793
SCALE = QH ** -0.5
XSCALE = 128 ** -0.5
Q_ORDER = [1, 2, 0]
NEG = -1e30

G_PRE_MIX, G_POST_MIX, G_PRE_X, G_POST_X, G_MEM, G_PRE_FFN, G_POST_FFN, B_CONV = range(0, 128, 16)
W_CONV, B_RG, B_IG, LAM, G_CKV = 128, 192, 208, 224, 240
W_F, B_F = 256, 640


class Phase:

    def __init__(self, after, trips, ends):
        self.trips, self.ends, self.n = trips, ends, len(ends)
        self.p0 = after.p_end if after else 0
        self.t0 = after.t_end if after else 0
        self.g0 = after.g_end if after else 0
        self.used, self.done, g = [], [], 0
        for e in ends:
            self.done += [g + j + 1 for j in range(e)]
            g += max(e, 1)
            self.used.append(g)
        self.steps, self.tiles = g, sum(ends)
        self.p_end = self.p0 + self.n * trips
        self.t_end = self.t0 + self.tiles * trips
        self.g_end = self.g0 + self.steps * trips
        assert self.n % SLOTS == 0

    def p(self, i, c):
        return i * self.n + self.p0 + c

    def t(self, i, j):
        return i * self.tiles + self.t0 + j

    def g(self, i, off):
        return i * self.steps + self.g0 + off

    def landed(self, i, c):
        return i * (16 * self.n // SLOTS) + 16 * ((self.p0 + c) // SLOTS + 1)


class Tally:

    def __init__(self, eng, sem):
        self.eng, self.sem, self.n, self.off = eng, sem, 0, 0

    def mark(self, ins):
        ins.then_inc(self.sem, 1)
        self.n += 1
        return ins

    def now(self):
        return self.off + self.n

    def wait(self):
        self.eng.wait_ge(self.sem, self.now())

    def link(self, ins):
        self.mark(ins)
        self.wait()


PH_A = Phase(None, 1, [0] * 7 + [5])
PH_Q0 = Phase(PH_A, 1, [0, 0, 0, 3])
PH_UKV = Phase(PH_Q0, 2, [4] * 4)
PH_Q = Phase(PH_UKV, HEADS // 2 - 1, [0, 0, 0, 3])
PH_GM = Phase(PH_Q, 4, [0, 2, 0, 2])
PH_OM = Phase(PH_GM, 4, [0, 2, 0, 2])
PH_LRU = Phase(PH_OM, 8, [0, 2, 0, 2])
PH_OL = Phase(PH_LRU, 8, [0, 2, 0, 2])
PH_WO = Phase(PH_OL, 4, [0, 2, 0, 2])
PH_CK = Phase(PH_WO, 1, [0, 2, 0, 2])
PH_CV = Phase(PH_CK, 1, [0, 2, 0, 2])
PH_CQ = Phase(PH_CV, 1, [0, 2, 0, 2])
PH_CO = Phase(PH_CQ, 1, [4] * 4)
PH_UP, PH_DN, _last = [], [], PH_CO
for _first, _count in GROUPS:
    PH_UP.append(Phase(_last, _count // 2, [0, 2, 0, 2]))
    PH_DN.append(Phase(PH_UP[-1], KT // 4, [1] * 4))
    _last = PH_DN[-1]
PIECES = _last.p_end


def build(nc, a, out):
    def w3(ap):
        return ap.rearrange("(k p) c -> p k c", p=P)

    w_in, w_ukv, w_om, w_ol, w_out = (w3(a[n][0]) for n in ("w_in", "w_ukv", "w_o_mla", "w_o_lru", "w_out"))
    w_ck, w_cv, w_cq, w_co = (w3(a[n][0]) for n in ("w_ck", "w_cv", "w_cq", "w_co"))
    w_up, w_dn = w3(a["w_up"][0]), w3(a["w_down"][0])
    w_rg = a["w_rg"][0].rearrange("b i j -> i b j")
    w_ig = a["w_ig"][0].rearrange("b i j -> i b j")
    x_tok = a["x"][0].rearrange("(m p) d -> p m d", p=P)
    mem_tok = a["mem"][0].rearrange("(m p) d -> p m d", p=P)
    out_tok = out[0].rearrange("(m p) d -> p m d", p=P)

    with ExitStack() as ctx:
        def sb(name, shape, dt=F32):
            return ctx.enter_context(nc.sbuf_tensor(name, shape, dt))

        def sem(name):
            return ctx.enter_context(nc.semaphore(name))

        raw = sb("raw", [P, SLOTS, 2048])
        wsp = sb("wsp", [P, SLOTS, 2, 2048], F32R)
        hsp = sb("hsp", [P, KT, 2 * T], F32R)
        asp = sb("asp", [P, KT, 2 * T], F32R)
        big_a = sb("big_a", [P, KT, T])
        big_b = sb("big_b", [P, KT, T])
        scr = sb("scr", [P, 4096])
        cr = sb("cr", [P, 4, T])
        par = sb("par", [P, 6 * P])
        ident = sb("ident", [P, P])
        ones = sb("ones", [P, P])
        rotm = sb("rotm", [P, P])
        mask = sb("mask", [P, 3 * P])
        pos_i = sb("pos_i", [P, T], I32)
        invf = sb("invf", [P, 1])
        cur = sb("cur", [P, 512])
        st = sb("st", [P, 96])
        ps = ctx.enter_context(nc.psum_tensor("ps", [P, 8, 512], F32))

        def s(c, n=1):
            return scr[:, c * T:(c + n) * T]

        a_tok = big_a[:, :, :].rearrange("p (m k) t -> p m (k t)", m=2)
        b_tok = big_b[:, :, :].rearrange("p (m k) t -> p m (k t)", m=2)
        out_sb = raw[:, 0:2, :]
        PROW = scr[:, 0:6 * P].rearrange("p (t c) -> p t c", c=P)
        CKV = [s(j) for j in range(RT)]
        KRAW, KR, COS, SIN = s(4), s(5), s(6), s(7)
        RV, RS = s(8), s(9)
        SQ = [s(10 + j) for j in range(4)]
        PR = [scr[:, 384 * e:384 * e + 384] for e in range(2)]
        PT = [scr[:, 2048 + 384 * e:2048 + 384 * e + 384] for e in range(2)]
        QRAW, QROPE, ROTT = s(11), s(12), s(13)
        QN = [s(14), s(15)]
        VC = scr[:, 768:1280].rearrange("p (m e d) -> p m e d", m=2, e=2)
        KC = [cur[:, e * T:(e + 1) * T] for e in range(2)]
        GW = cur[:, :].rearrange("p (g e j) -> p g e j", g=2, e=2)
        XR, XC, RG, IG = ([s(n), s(n + 1)] for n in (0, 2, 4, 6))
        TH, SQT, RC, YY = ([s(n), s(n + 1)] for n in (8, 10, 12, 14))
        OL_O, OL_G = [s(0), s(1)], [s(2), s(3)]
        CVT = scr[:, 0:4 * T].rearrange("p (m d) -> p m d", m=2)
        CKT = [s(12 + j) for j in range(4)]
        ACC, ACS = s(4), [s(5), s(6)]
        RT0, RR = s(10), s(11)
        CQ = [big_a[:, j, :] for j in range(XH)]
        XP = [big_a[:, n:n + 2, :] for n in (4, 6, 8, 10)]
        XPT = [big_a[:, n:n + 2, :] for n in (12, 14, 0, 2)]
        UR, UC = [s(0), s(1), s(4), s(5)], [s(2), s(3), s(6), s(7)]
        HID = [s(12), s(13)]

        landed = [sem(f"landed{n}") for n in range(SLOTS)]
        hi_done, lo_done, gemm_step = sem("hi_done"), sem("lo_done"), sem("gemm_step")
        cross_done, tile_out = sem("cross_done"), sem("tile_out")
        dve_self, pool_self = sem("dve_self"), sem("pool_self")
        x_in = [sem("x_in0"), sem("x_in1")]
        par_in, pos_in, gate_w_in, mem_in, x2_in = (
            sem(n) for n in ("par_in", "pos_in", "gate_w_in", "mem_in", "x2_in"))
        out_stored = sem("out_stored")
        consts_made, prow_zero, mask_made = sem("consts_made"), sem("prow_zero"), sem("mask_made")
        lam_exp, kv_cur = sem("lam_exp"), sem("kv_cur")
        par_turned, par_ready = sem("par_turned"), sem("par_ready")
        x_sq, x_scaled, x_turned, x_hi, x_lo = (sem(n) for n in ("x_sq", "x_scaled", "x_turned", "x_hi", "x_lo"))
        ckv_sq, ckv_sum, ckv_norm, ckv_hi, ckv_lo = (
            sem(n) for n in ("ckv_sq", "ckv_sum", "ckv_norm", "ckv_hi", "ckv_lo"))
        var_ready, root_ready = sem("var_ready"), sem("root_ready")
        angle_ready, table_ready = sem("angle_ready"), sem("table_ready")
        rot_done, roped = sem("rot_done"), sem("roped")
        scores_done, neg_max, exps_done, sums_inv, probs_ready, probs_turned, probs_copied, pv_done, o_hi, o_lo = (
            sem(n) for n in ("scores_done", "neg_max", "exps_done", "sums_inv", "probs_ready", "probs_turned",
                             "probs_copied", "pv_done", "o_hi", "o_lo"))
        gate_done = sem("gate_done")
        conv_done, gates_mm, gates_act, lru_t, lru_root, lru_a, lru_scan, y_act, hrg, hrg_hi, hrg_lo = (
            sem(n) for n in ("conv_done", "gates_mm", "gates_act", "lru_t", "lru_root", "lru_a", "lru_scan",
                             "y_act", "hrg", "hrg_hi", "hrg_lo"))
        lru_rc = sem("lru_rc")
        olg_sig, merged_out, m_hi, m_lo = sem("olg_sig"), sem("merged_out"), sem("m_hi"), sem("m_lo")
        mem_sq, mem_scaled, mem_turned, mem_hi, mem_lo = (
            sem(n) for n in ("mem_sq", "mem_scaled", "mem_turned", "mem_hi", "mem_lo"))
        ysq_done, norm_sum, rms_ready = sem("ysq_done"), sem("norm_sum"), sem("rms_ready")
        y_scaled, xt_turned, res_out, sq_made, res_hi, res_lo = (
            sem(n) for n in ("y_scaled", "xt_turned", "res_out", "sq_made", "res_hi", "res_lo"))
        up_ready, up_bias, up_conv, gelu_done, hid_out, hid_hi, hid_lo = (
            sem(n) for n in ("up_ready", "up_bias", "up_conv", "gelu_done", "hid_out", "hid_hi", "hid_lo"))
        fin_turned, fin_copied = sem("fin_turned"), sem("fin_copied")

        def xst(h, n):
            at = 64 + 8 * h + 2 * n
            return st[:, at:at + 2]

        def col(base, m):
            return par[:, bass.ds(m + base, 1)]

        def piece_size(ph, c):
            if ph is PH_A:
                return 2 * (RANK + ROPE) if c < ph.n else 8 * QH
            if ph is PH_Q0 and c < ph.n:
                return 8 * QH
            return 2048

        block = ctx.enter_context(nc.Block())

        def rounds(eng, ph, body, first_apart=False, last_apart=False):
            first, n = int(first_apart), ph.trips - last_apart
            if first_apart:
                body(0)
            if n - first == 1:
                body(first)
            else:
                with eng.Fori(first, n) as i:
                    body(i)
            if last_apart:
                body(ph.trips - 1)

        @block.sync
        def _(sp):
            def piece(ph, i, c, k, cols, src):
                if not isinstance(i, int) or ph.p(i, c) >= SLOTS:
                    sp.wait_ge(lo_done, ph.p(i, c) - SLOTS + 1)
                slot = (ph.p0 + c) % SLOTS
                dst = raw[:, slot, 0:k * cols].rearrange("p (k c) -> p k c", k=k)
                sp.dma_start(dst, src).then_inc(landed[slot], 16)

            def wide(ph, i, c, w, col):
                h = KT // 2
                piece(ph, i, c, h, T, w[:, (c % 2) * h:(c % 2) * h + h, bass.ds(col, T)])

            def plain(ph, w, base=0):
                def body(i):
                    for c in range(4):
                        wide(ph, i, c, w, i * 512 + base + (c // 2) * T)
                rounds(sp, ph, body)

            def q_cols(ph, unit0):
                def body(i):
                    for c in range(4):
                        piece(ph, i, c, 4, 2 * QH, w_in[:, 4 * c:4 * c + 4, bass.ds(i * (2 * QH) + unit0 * 2 * QH, 2 * QH)])
                rounds(sp, ph, body)

            sp.dma_start(a_tok[:, 0, :], x_tok[:, 0, :]).then_inc(x_in[0], 16)
            sp.wait_ge(prow_zero, 1)
            rows = [(0, G_PRE_MIX, "g_pre_mix"), (0, G_POST_MIX, "g_post_mix"), (0, G_PRE_X, "g_pre_x"),
                    (0, G_POST_X, "g_post_x"), (0, G_MEM, "g_mem"), (0, G_PRE_FFN, "g_pre_ffn"),
                    (0, G_POST_FFN, "g_post_ffn"), (0, B_CONV, "b_conv_lru"), (1, 0, "w_conv_lru"),
                    (1, B_RG - P, "b_rg"), (1, B_IG - P, "b_ig"), (1, LAM - P, "lru_lambda"), (1, G_CKV - P, "g_ckv"),
                    (2, 0, "w_fconv"), (5, 0, "b_fconv")]
            for tile, at, name in rows:
                src = a[name]
                if name == "w_fconv":
                    for kk in range(3):
                        sp.dma_start(PROW[0:2 * FT, tile + kk, :], src[0, kk].rearrange("(r c) -> r c", c=P)).then_inc(par_in, 16)
                    continue
                if name == "w_conv_lru":
                    src = src[0].rearrange("k (r c) -> (k r) c", c=P)
                elif name in ("b_rg", "b_ig"):
                    src = src[0]
                else:
                    src = src[0].rearrange("(r c) -> r c", c=P)
                n = src.shape[0]
                sp.dma_start(PROW[at:at + n, tile, :], src).then_inc(par_in, 16)
            sp.dma_start(pos_i[:, :], a["positions"].to_broadcast([P, T])).then_inc(pos_in, 16)
            sp.dma_start(invf[:, :], a["inv_freq"]).then_inc(pos_in, 16)
            for c in range(8):
                piece(PH_A, 0, c, 2, RANK + ROPE, w_in[:, 2 * c:2 * c + 2, OFF_CKV:OFF_LX])
            q_cols(PH_Q0, 0)

            def ukv(i):
                for c in range(4):
                    piece(PH_UKV, i, c, RT, 512, w_ukv[:, :, bass.ds(i * 2048 + c * 512, 512)])
            rounds(sp, PH_UKV, ukv)
            q_cols(PH_Q, 1)
            plain(PH_GM, w_in, OFF_GM)
            plain(PH_OM, w_om)

            def lru(i):
                for c in range(4):
                    wide(PH_LRU, i, c, w_in, i * T + (OFF_LX if c < 2 else OFF_LY))
            rounds(sp, PH_LRU, lru)

            def o_lru(i):
                for c in range(4):
                    if c < 2:
                        wide(PH_OL, i, c, w_in, i * T + OFF_GL)
                    else:
                        wide(PH_OL, i, c, w_ol, i * 2 * P)
            rounds(sp, PH_OL, o_lru)
            plain(PH_WO, w_out)
            plain(PH_CK, w_ck)
            plain(PH_CV, w_cv)
            plain(PH_CQ, w_cq)
            for c in range(4):
                piece(PH_CO, 0, c, 4, 512, w_co[:, :, c * 512:(c + 1) * 512])
            for (f0, fn), up, dn in zip(GROUPS, PH_UP, PH_DN):
                def up_cols(i):
                    for c in range(4):
                        wide(up, i, c, w_up, i * T + f0 * P + (0 if c < 2 else DFF))
                rounds(sp, up, up_cols)

                def dn_cols(i):
                    for c in range(4):
                        piece(dn, i, c, fn, P, w_dn[:, f0:f0 + fn, bass.ds(i * 512 + c * P, P)])
                rounds(sp, dn, dn_cols)
            for kq in range(4):
                sp.wait_ge(fin_copied, 2 * kq + 2)
                cols = slice(kq * 512, (kq + 1) * 512)
                sp.dma_start(out_tok[:, :, cols], out_sb[:, :, cols]).then_inc(out_stored, 16)
            sp.wait_ge(out_stored, 64)

        @block.tensor
        def _(pe):
            last_in = {}

            def enter(ph, banks):
                need = max([last_in[b] + 1 for n, b in enumerate(banks)
                            if b in last_in and last_in[b] > ph.t0 + n - len(banks)] or [0])
                if need:
                    pe.wait_ge(tile_out, need)
                for n, b in enumerate(banks):
                    last_in[b] = ph.t_end - len(banks) + n

            def claim(ph, i, j, back=4):
                if not isinstance(i, int) or ph.t(i, j) >= back:
                    pe.wait_ge(tile_out, ph.t(i, j) + 1 - back)

            def arrive(ph, i, c):
                pe.wait_ge(lo_done, ph.p(i, c) + 1)

            def feature_tile(ph, i, c, j, bank, slot, lhs, k0, kn, src, first, last, note):
                for k in range(kn):
                    x = src[:, k0 + k, :]
                    f, l = first and k == 0, last and k == kn - 1
                    parts = [1, 0] if l and not f else [0, 1]
                    for n, part in enumerate(parts):
                        w = T if part else 2 * T
                        mm = pe.matmul(ps[:, bank, 0:w], lhs(part, k), x[:, 0:w], start=(f and part == 0),
                                       stop=(l and n == 1))
                if note:
                    mm.then_inc(gemm_step, 1)

            def token_tile(ph, bank, m, rhs, k0, kn, src, first, last, note):
                for k in range(kn):
                    f, l = first and k == 0, last and k == kn - 1
                    parts = [1, 0] if l and not f else [0, 1]
                    for n, part in enumerate(parts):
                        x = src[:, k0 + k, part * T + m * P:part * T + m * P + P]
                        if part:
                            o, r = ps[:, bank, 0:T], rhs(k, False)
                        else:
                            o, r = ps[:, bank, :], rhs(k, True)
                        mm = pe.matmul(o, x, r, start=(f and part == 0), stop=(l and n == 1))
                if note:
                    mm.then_inc(gemm_step, 1)

            def wtile(slot, part, kn, k, c0, cn=P):
                return wsp[:, slot, part, 0:2048 // kn * kn].rearrange("p (k c) -> p k c", k=kn)[:, k, c0:c0 + cn]

            def wide_piece(ph, i, c, src, ready=None, paced=False):
                u, h = c // 2, c % 2
                arrive(ph, i, c)
                order = [(j, k) for k in range(8) for j in range(2)] if paced else [(j, k) for j in range(2) for k in range(8)]
                for j, k in order:
                    if k == 0 and h == 0:
                        claim(ph, i, 2 * u + j)
                    if ready and j == 0:
                        ready(8 * h + k)
                    f, l = h == 0 and k == 0, h == 1 and k == 7
                    feature_tile(ph, i, c, 2 * u + j, 2 * u + j, c, lambda part, _, k=k, j=j: wtile(c, part, 8, k, j * P),
                                 8 * h + k, 1, src, f, l, l or (h == 0 and j == 1 and k == 7))

            def wide_unit(ph, i, u, src, between=None, ready=None):
                for c in (2 * u, 2 * u + 1):
                    wide_piece(ph, i, c, src, ready, paced=ready is not None)
                    if between:
                        between(c)

            def plain(ph, src):
                enter(ph, [0, 1, 2, 3])

                def body(i):
                    for u in range(2):
                        wide_unit(ph, i, u, src)
                rounds(pe, ph, body)

            pe.wait_ge(consts_made, 4)
            pe.wait_ge(par_in, 16 * 17)
            for n in range(6):
                mm = pe.transpose(ps[:, 4 + n // 4, (n % 4) * P:(n % 4 + 1) * P], PROW[:, n, :], ident[:, :])
                mm.then_inc(par_turned, 1)

            def turn(src_tok, k, bank, col, done):
                for m in range(2):
                    mm = pe.transpose(ps[:, bank, col + m * P:col + (m + 1) * P], src_tok[:, m, k * P:(k + 1) * P], ident[:, :])
                mm.then_inc(done, 1)

            pe.wait_ge(x_scaled, 2)
            pe.wait_ge(par_ready, 2)
            for k in range(KT):
                turn(a_tok, k, k // 2, (k % 2) * T, x_turned)

            for c in range(8):
                arrive(PH_A, 0, c)
                slot = c % SLOTS
                wv = [wsp[:, slot, part, 0:2 * (RANK + ROPE)].rearrange("p (k c) -> p k c", k=2) for part in range(2)]
                for k in range(2):
                    pe.wait_ge(x_lo, 2 * c + k + 1)
                for j in range(5):
                    if c == 0:
                        pe.wait_ge(x_lo, 2 * j + 2)
                    for k in range(2):
                        def lhs(part, _, k=k, j=j):
                            at = min(j * P, RANK + ROPE - P)
                            return wv[part][:, k, at:at + P]
                        f, l = c == 0 and k == 0, c == 7 and k == 1
                        feature_tile(PH_A, 0, c, j, j, slot, lhs, 2 * c + k, 1, hsp, f, l, l or (c < 7 and j == 4 and k == 1))

            def q_piece(ph, i, c):
                arrive(ph, i, c)
                for n, j in enumerate(Q_ORDER):
                    if c == 0:
                        claim(ph, i, n, 3)

                    def lhs(part, k):
                        w = wsp[:, c % SLOTS, part, 0:8 * QH].rearrange("p (k c) -> p k c", k=4)
                        return w[:, k, j * P:(j + 1) * P]
                    feature_tile(ph, i, c, n, j, c % SLOTS, lhs, 4 * c, 4, hsp, c == 0, c == 3, c == 3 or n == 2)

            def ckv_stats():
                pe.wait_ge(ckv_sq, RT)
                for j in range(RT):
                    mm = pe.matmul(ps[:, 5, 0:T], ones[:, :], SQ[j], start=(j == 0), stop=(j == RT - 1))
                mm.then_inc(ckv_sum, 1)
                pe.wait_ge(tile_out, 5)
                pe.matmul(ps[:, 6, 0:T], rotm[:, :], KRAW, start=True, stop=True).then_inc(rot_done, 1)

            for j in range(5):
                last_in[j] = j
            enter(PH_Q0, Q_ORDER)
            q_piece(PH_Q0, 0, 0)
            ckv_stats()
            for c in range(1, 4):
                q_piece(PH_Q0, 0, c)

            def ukv(i):
                for c in range(4):
                    arrive(PH_UKV, i, c)
                    wv = [wsp[:, c, part, :].rearrange("p (k e c) -> p k e c", k=RT, e=2) for part in range(2)]
                    for j in range(2):
                        claim(PH_UKV, i, 4 * c + j)
                        feature_tile(PH_UKV, i, c, j, j, c, lambda part, k: wv[part][:, k, j, 0:P], 0, RT, asp,
                                     True, True, True)
                    both = wsp[:, c, :, :].rearrange("p h (k e c) -> p h k e c", k=RT, e=2)
                    for m in range(2):
                        claim(PH_UKV, i, 4 * c + 2 + m)

                        def rhs(k, two):
                            return both[:, :, k, :, P:2 * P] if two else wv[0][:, k, :, P:2 * P]
                        token_tile(PH_UKV, 2 + m, m, rhs, 0, RT, asp, True, True, True)
            pe.wait_ge(ckv_lo, RT)
            enter(PH_UKV, [0, 1, 2, 3])
            rounds(pe, PH_UKV, ukv)

            def attention(u, between):
                between(0)
                pe.wait_ge(tile_out, PH_Q.t(u, 0) - 1)
                pe.wait_ge(roped, u + 1)
                if not isinstance(u, int) or u:
                    pe.wait_ge(o_lo, u)
                pe.matmul(ps[:, 6, 0:T], rotm[:, :], QRAW, start=True, stop=True).then_inc(rot_done, 1)
                between(1)
                pe.wait_ge(roped, u + 2)
                pe.wait_ge(kv_cur, u * 2 + 2)
                for e in range(2):
                    rope = slice(64 * e, 64 * e + 64)
                    for q in range(2):
                        kn = P * (q + 1)
                        o = ps[:, 3 + e, P * q:P * q + kn]
                        pe.matmul(o, QN[e][:, q * P:(q + 1) * P], KC[e][:, 0:kn], start=True, stop=False)
                        mm = pe.matmul(o, QROPE[rope, q * P:(q + 1) * P], KR[rope, 0:kn], start=False, stop=True)
                    mm.then_inc(scores_done, 1)
                between(2)
                for e in range(2):
                    pe.wait_ge(probs_ready, u * 4 + 2 * e + 2)
                    for b in range(3):
                        mm = pe.transpose(ps[:, 5 + 2 * e, b * P:(b + 1) * P], PR[e][:, b * P:(b + 1) * P], ident[:, :])
                    mm.then_inc(probs_turned, 1)
                between(3)
                for e in range(2):
                    pe.wait_ge(probs_copied, u * 2 + e + 1)
                    o = ps[:, 6, e * T:(e + 1) * T]
                    pe.matmul(o, VC[:, 0, e, :], PT[e][:, 0:2 * P], start=True, stop=False)
                    mm = pe.matmul(o[:, P:2 * P], VC[:, 1, e, :], PT[e][:, 2 * P:3 * P], start=False, stop=True)
                mm.then_inc(pv_done, 1)

            enter(PH_Q, Q_ORDER)
            pe.wait_ge(tile_out, PH_UKV.t_end)
            rounds(pe, PH_Q, lambda i: attention(i, lambda c: q_piece(PH_Q, i, c)), first_apart=True)
            enter(PH_GM, [0, 1, 2, 3])


            def scores_read(k):
                if k == 7:
                    pe.wait_ge(neg_max, HEADS)
            attention(HEADS // 2 - 1,
                      lambda c: wide_piece(PH_GM, 0, c, hsp, ready=scores_read if c == 2 else None))
            with pe.Fori(1, PH_GM.trips) as i:
                for c in range(4):
                    wide_piece(PH_GM, i, c, hsp)
            pe.wait_ge(o_lo, HEADS // 2)
            plain(PH_OM, asp)

            enter(PH_LRU, [0, 1, 2, 3])

            def lru(i):
                def gates(c):
                    if c != 2:
                        return
                    pe.wait_ge(gate_w_in, i * 32 + 32)
                    for e in range(2):
                        pe.wait_ge(conv_done, i * 2 + e + 1)
                        if not isinstance(i, int) or i:
                            pe.wait_ge(gates_act, i * 4)
                        for g in range(2):
                            mm = pe.matmul(ps[:, 4 + e, g * T:(g + 1) * T], GW[:, g, e, :], XC[e], start=True, stop=True)
                        mm.then_inc(gates_mm, 1)
                wide_unit(PH_LRU, i, 0, hsp)
                wide_unit(PH_LRU, i, 1, hsp, between=gates)
            rounds(pe, PH_LRU, lru, first_apart=True)

            enter(PH_OL, [0, 1, 2, 3])

            def o_lru(i):
                wide_unit(PH_OL, i, 0, hsp)
                pe.wait_ge(hrg_lo, KT)
                wide_unit(PH_OL, i, 1, asp)
            rounds(pe, PH_OL, o_lru)

            enter(PH_WO, [0, 1, 2, 3])
            pe.wait_ge(mem_scaled, 2)

            def turn_mem(c):
                if c in (0, 2):
                    for k in range(4 * c, 4 * c + 8):
                        if c and k % 2 == 0:
                            pe.wait_ge(mem_lo, k - 6)
                        turn(b_tok, k, 4 + k // 2 % 4, (k % 2) * T, mem_turned)

            def m_ready(k):
                if k % 2 == 0:
                    pe.wait_ge(m_lo, k // 2 + 1)
            wide_unit(PH_WO, 0, 0, hsp, between=turn_mem, ready=m_ready)
            wide_unit(PH_WO, 0, 1, hsp, between=turn_mem)
            with pe.Fori(1, PH_WO.trips) as i:
                for u in range(2):
                    wide_unit(PH_WO, i, u, hsp)

            def norm(count):
                pe.wait_ge(ysq_done, count)
                pe.matmul(ps[:, 4, 0:T], ones[:, :], ACC, start=True, stop=True).then_inc(norm_sum, 1)


            def turn_x(ph_n, c):
                for k in range(*RES_AT.get((ph_n, c), (0, 0))):
                    if k == 0:
                        pe.wait_ge(x2_in, 16)
                    if k >= 3:
                        pe.wait_ge(res_out, k - 2)
                    turn(a_tok, k, 5 + k % 3, 0, xt_turned)

            def ck_between(c):
                if c == 0:
                    norm(KT)
                turn_x(0, c)
            enter(PH_CK, [0, 1, 2, 3])
            pe.wait_ge(mem_lo, KT)
            for u in range(2):
                wide_unit(PH_CK, 0, u, asp, between=ck_between)

            enter(PH_CV, [0, 1, 2, 3])
            for c in range(4):
                arrive(PH_CV, 0, c)
                u, h = c // 2, c % 2
                for m in range(2):
                    if h == 0:
                        claim(PH_CV, 0, 2 * u + m)

                    def rhs(k, two):
                        both = wsp[:, c, :, :].rearrange("p h (k c) -> p h k c", k=8)
                        return both[:, :, k, :] if two else both[:, 0, k, :]
                    for k in range(8):
                        f, l = h == 0 and k == 0, h == 1 and k == 7
                        token_tile(PH_CV, 2 * u + m, m, lambda _, two, k=k: rhs(k, two), 8 * h + k, 1, asp, f, l,
                                   l or (h == 0 and m == 1 and k == 7))
                turn_x(1, c)

            enter(PH_CQ, [0, 1, 2, 3])
            for c in range(4):
                wide_piece(PH_CQ, 0, c, hsp, ready=lambda k: pe.wait_ge(res_lo, k + 1))
                if c == 2:
                    norm(2 * KT)

            def x_scores(h):
                pe.wait_ge(tile_out, PH_CQ.t(0, h) + 1)
                if h == 0:
                    pe.wait_ge(rms_ready, 5)
                for q in range(2):
                    mm = pe.matmul(ps[:, 4 + h, q * T:(q + 1) * T], CQ[h][:, q * P:(q + 1) * P], CKT[h],
                                   start=True, stop=True)
                mm.then_inc(scores_done, 1)

            def x_turn(h):
                pe.wait_ge(probs_ready, 32 + 2 * (h + 1))
                for m in range(2):
                    for q in range(2):
                        mm = pe.transpose(ps[:, h, m * T + q * P:m * T + (q + 1) * P],
                                          XP[h][:, q, m * P:(m + 1) * P], ident[:, :])
                mm.then_inc(probs_turned, 1)

            def x_pv(h):
                pe.wait_ge(probs_copied, HEADS + h + 1)
                for m in range(2):
                    mm = pe.matmul(ps[:, 4 + h, 0:T], CVT[:, m, h * P:(h + 1) * P], XPT[h][:, m, :],
                                   start=(m == 0), stop=(m == 1))
                mm.then_inc(pv_done, 1)
            for h in range(XH - 1):
                x_scores(h)
            x_turn(0)
            x_scores(XH - 1)
            for h in range(XH):
                if h + 1 < XH:
                    x_turn(h + 1)
                x_pv(h)

            enter(PH_CO, [0, 1, 2, 3])
            pe.wait_ge(o_lo, HEADS // 2 + XH)
            for c in range(4):
                arrive(PH_CO, 0, c)
                for j in range(4):
                    claim(PH_CO, 0, 4 * c + j)
                    feature_tile(PH_CO, 0, c, 4 * c + j, j, c, lambda part, k: wtile(c, part, 4, k, j * P),
                                 0, XH, asp, True, True, True)
            norm(3 * KT)

            for n, ((f0, fn), up, dn) in enumerate(zip(GROUPS, PH_UP, PH_DN)):
                enter(up, [0, 1, 2, 3])

                def up_round(i, first=False):
                    def x2_sum(c):
                        if c == 3:
                            norm(4 * KT)

                    def x2_ready(k):
                        pe.wait_ge(res_lo, KT + k + 1)
                    wide_unit(up, i, 0, hsp, ready=x2_ready if first else None)
                    wide_unit(up, i, 1, hsp, between=x2_sum if first else None)
                if n == 0:
                    up_round(0, True)
                    with pe.Fori(1, up.trips) as i:
                        up_round(i)
                else:
                    rounds(pe, up, up_round)

                enter(dn, [0, 1, 2, 3])

                def dn_part(i, c, ks):
                    arrive(dn, i, c)
                    if ks[0] == 0:
                        claim(dn, i, c)
                    for k in ks:
                        wv = [wsp[:, c, part, 0:fn * P].rearrange("p (k c) -> p k c", k=fn) for part in range(2)]
                        feature_tile(dn, i, c, c, c, c, lambda part, _, k=k: wv[part][:, k, :], k, 1, asp, k == 0,
                                     k == fn - 1, k == fn - 1)

                def dn_round(i):
                    if isinstance(i, int):
                        pe.wait_ge(hid_lo, f0 + fn - 2)
                        for c in range(2):
                            dn_part(i, c, range(fn - 2))
                        pe.wait_ge(hid_lo, f0 + fn)
                        for c in range(2):
                            dn_part(i, c, range(fn - 2, fn))
                    for c in range(2 if isinstance(i, int) else 0, 4):
                        dn_part(i, c, range(fn))
                rounds(pe, dn, dn_round, first_apart=True)
            norm(5 * KT)

            for kq in range(4):
                pe.wait_ge(res_out, 2 * KT + 4 * kq + 4)
                for m in range(2):
                    for k in range(4 * kq, 4 * kq + 4):
                        mm = pe.transpose(ps[:, 2 * kq + m, (k % 4) * P:(k % 4 + 1) * P],
                                          big_b[:, k, m * P:(m + 1) * P], ident[:, :])
                    mm.then_inc(fin_turned, 1)

        @block.scalar
        def _(act):
            act.dma_start(a_tok[:, 1, :], x_tok[:, 1, :]).then_inc(x_in[1], 16)

            def root(n, out_, in_, scale=1.0):
                act.wait_ge(var_ready, n)
                act.activation(out_, in_, ACT.Sqrt, scale=scale).then_inc(root_ready, 1)

            def hi(ph, i, c):
                p0 = ph.p0 + c
                if isinstance(i, int) and ph.p(i, c) >= PIECES:
                    return
                if c >= SLOTS and c - SLOTS < ph.n:
                    act.wait_ge(gemm_step, ph.g(i, ph.used[c - SLOTS]))
                elif not isinstance(i, int) or ph.g(i, 0) > 0:
                    act.wait_ge(gemm_step, ph.g(i, 0))
                act.wait_ge(landed[p0 % SLOTS], ph.landed(i, c))
                n = piece_size(ph, c)
                act.activation(wsp[:, p0 % SLOTS, 0, 0:n], raw[:, p0 % SLOTS, 0:n], ACT.Copy).then_inc(hi_done, 1)

            def cross(ph, i, j, slot=None, bank=None, scaled=None):
                slot = j % 4 if slot is None else slot
                bank = j % 4 if bank is None else bank
                act.wait_ge(gemm_step, ph.g(i, ph.done[j]))
                if not isinstance(i, int) or ph.t(i, j) >= 3:
                    act.wait_ge(tile_out, ph.t(i, j) - 2)
                if scaled is not None:
                    act.wait_ge(up_ready, scaled)
                act.activation(cr[:, slot, :], ps[:, bank, T:2 * T], ACT.Copy).then_inc(cross_done, 1)

            def plain(ph):
                def body(i):
                    for c in range(4):
                        hi(ph, i, c + LEAD)
                        if c % 2:
                            for e in range(2):
                                cross(ph, i, c - 1 + e)
                rounds(act, ph, body)

            for m in range(2):
                act.wait_ge(x_in[m], 16)
                act.activation(b_tok[:, m, :], a_tok[:, m, :], ACT.Square, accum_out=st[:, m:m + 1]).then_inc(x_sq, 1)
            root(1, st[:, 4:6], st[:, 2:4])
            act.wait_ge(rms_ready, 1)
            act.activation(a_tok[:, 1, :], a_tok[:, 1, :], ACT.Copy, scale=st[:, 27:28]).then_inc(x_scaled, 1)
            for p in range(LEAD):
                hi(PH_A, 0, p)
            act.wait_ge(par_ready, 4)
            act.activation(st[:, 48:64], st[:, 32:48], ACT.Exp, scale=-1.0).then_inc(lam_exp, 1)
            for k in range(KT):
                act.wait_ge(x_turned, k - k % 2 + 2)
                act.activation(hsp[:, k, 0:T], ps[:, k // 2, (k % 2) * T:(k % 2 + 1) * T], ACT.Copy,
                               scale=par[:, G_PRE_MIX + k:G_PRE_MIX + k + 1]).then_inc(x_hi, 1)
            for c in range(8):
                hi(PH_A, 0, c + LEAD)
            for j in range(5):
                cross(PH_A, 0, j, slot=(j + 3) % 4, bank=j)
            for j in range(RT):
                act.wait_ge(tile_out, j + 1)
                act.activation(SQ[j], CKV[j], ACT.Square).then_inc(ckv_sq, 1)
            hi(PH_Q0, 0, 2)
            root(2, RS, RV)
            hi(PH_Q0, 0, 3)
            act.wait_ge(angle_ready, 2)
            act.activation(SIN, SIN, ACT.Sin).then_inc(table_ready, 1)
            act.activation(COS, COS, ACT.Sin).then_inc(table_ready, 1)
            for j in range(RT):
                act.wait_ge(ckv_norm, j + 1)
                act.activation(asp[:, j, 0:T], CKV[j], ACT.Copy,
                               scale=par[:, G_CKV + j:G_CKV + j + 1]).then_inc(ckv_hi, 1)
            hi(PH_Q0, 0, 4)
            hi(PH_Q0, 0, 5)
            for n, b in enumerate(Q_ORDER):
                cross(PH_Q0, 0, n, slot=n, bank=b)

            def ukv(i):
                for c in range(4):
                    hi(PH_UKV, i, c + LEAD)
                    for j in range(4):
                        cross(PH_UKV, i, 4 * c + j)
            rounds(act, PH_UKV, ukv)

            def attention(u, ph, i, between):
                hi(ph, i, 2)
                hi(ph, i, 3)
                for e in range(2):
                    act.wait_ge(neg_max, u * 2 + e + 1)
                    for q in range(2):
                        n = 2 * e + q
                        blk = PR[e][:, P * q:P * q + P * (q + 1)]
                        act.activation(blk, blk, ACT.Exp, bias=st[:, 12 + n:13 + n],
                                       accum_out=st[:, 16 + n:17 + n]).then_inc(exps_done, 1)
                between(0)
                hi(ph, i, 4)
                for e in range(2):
                    act.wait_ge(probs_turned, u * 2 + e + 1)
                    act.activation(PT[e], ps[:, 5 + 2 * e, 0:384], ACT.Copy).then_inc(probs_copied, 1)
                hi(ph, i, 5)
                between(1)
                act.wait_ge(pv_done, u + 1)
                act.activation(asp[:, bass.ds(u * 2, 2), 0:T], ps[:, 6, :].rearrange("p (e t) -> p e t", e=2),
                               ACT.Copy).then_inc(o_hi, 1)

            def q_tiles(i, part):
                if part:
                    for n, b in enumerate(Q_ORDER):
                        cross(PH_Q, i, n, slot=n, bank=b)
            rounds(act, PH_Q, lambda i: attention(i, PH_Q, i, lambda part: q_tiles(i, part)))

            def gm_tiles(i, part):
                for e in range(2):
                    cross(PH_GM, i, 2 * part + e)
                for e in range(2):
                    act.wait_ge(tile_out, PH_GM.t(i, 2 * part + e + 1))
                    m = big_a[:, bass.ds(i * 4 + 2 * part + e, 1), :].rearrange("p a t -> p (a t)")
                    act.activation(m, m, ACT.Sigmoid).then_inc(gate_done, 1)
            attention(HEADS // 2 - 1, PH_GM, 0, lambda part: gm_tiles(0, part))
            for m in range(2):
                act.dma_start(b_tok[:, m, :], mem_tok[:, m, :]).then_inc(mem_in, 16)
            for g, w in enumerate((w_rg, w_ig)):
                act.dma_start(GW[:, g, :, :], w[:, 0:2, :]).then_inc(gate_w_in, 16)

            with act.Fori(1, PH_GM.trips) as i:
                for part in range(2):
                    hi(PH_GM, i, 2 * part + 2)
                    hi(PH_GM, i, 2 * part + 3)
                    gm_tiles(i, part)
            act.wait_ge(mem_in, 32)
            for m in range(2):
                act.activation(scr[:, 2048:4096], b_tok[:, m, :], ACT.Square, accum_out=st[:, m:m + 1]).then_inc(mem_sq, 1)
                act.wait_ge(mem_sq, m + 1)
            root(3, st[:, 4:6], st[:, 2:4])
            plain(PH_OM)

            def y_gelu(i):
                for e in range(2):
                    act.wait_ge(tile_out, PH_LRU.t(i, 0) + 3 + e)
                    act.activation(YY[e], YY[e], ACT.Gelu_apprx_tanh).then_inc(y_act, 1)

            def y_hi(i):
                for e in range(2):
                    act.wait_ge(hrg, i * 2 + e + 1)
                    act.activation(asp[:, bass.ds(i * 2 + e, 1), 0:T].rearrange("p a t -> p (a t)"), YY[e],
                                   ACT.Copy).then_inc(hrg_hi, 1)

            def lru(i):
                ph = PH_LRU
                hi(ph, i, 2)
                if not isinstance(i, int) or i:
                    y_gelu(i - 1)
                hi(ph, i, 3)
                for e in range(2):
                    cross(ph, i, e)
                if not isinstance(i, int) or i:
                    y_hi(i - 1)
                hi(ph, i, 4)
                for e in range(2):
                    act.wait_ge(gates_mm, i * 2 + e + 1)
                    for g, (buf, b) in enumerate(((RG, B_RG), (IG, B_IG))):
                        act.activation(buf[e], ps[:, 4 + e, g * T:(g + 1) * T], ACT.Sigmoid,
                                       bias=par[:, bass.ds(i * 2 + b + e, 1)]).then_inc(gates_act, 1)
                for e in range(2):
                    act.wait_ge(gates_act, i * 4 + 2 * e + 2)
                    act.activation(TH[e], RG[e], ACT.Tanh, scale=par[:, bass.ds(i * 2 + LAM + e, 1)]).then_inc(lru_t, 1)
                for e in range(2):
                    act.wait_ge(lru_t, i * 2 + e + 1)
                    act.activation(SQT[e], TH[e], ACT.Sqrt, scale=4.0).then_inc(lru_root, 1)
                if not isinstance(i, int) or i < ph.trips - 1:
                    for g, w in enumerate((w_rg, w_ig)):
                        act.dma_start(GW[:, g, :, :], w[:, bass.ds(i * 2 + 2, 2), :]).then_inc(gate_w_in, 16)
                hi(ph, i, 5)
                for e in range(2):
                    cross(ph, i, 2 + e)
            rounds(act, PH_LRU, lru, first_apart=True, last_apart=True)
            y_gelu(PH_LRU.trips - 1)

            def merged_hi(pairs):
                for k in pairs:
                    act.wait_ge(gemm_step, PH_OL.g(PH_OL.trips - 1, PH_OL.used[1]))
                    act.wait_ge(merged_out, 2 * k + 2)
                    act.activation(hsp[:, 2 * k:2 * k + 2, 0:T], big_a[:, 2 * k:2 * k + 2, :], ACT.Copy).then_inc(m_hi, 1)

            def o_lru(i):
                first, last = (isinstance(i, int) and i == n for n in (0, PH_OL.trips - 1))
                for c in range(4):
                    hi(PH_OL, i, c + LEAD)
                    if first and c == 0:
                        y_hi(PH_LRU.trips - 1)
                    if last and c >= 2:
                        merged_hi(range(4) if c == 2 else range(4, 7))
                    if c % 2:
                        for e in range(2):
                            cross(PH_OL, i, c - 1 + e)
                    if c == 1:
                        for e in range(2):
                            act.wait_ge(tile_out, PH_OL.t(i, e) + 1)
                            act.activation(OL_G[e], OL_G[e], ACT.Sigmoid).then_inc(olg_sig, 1)
            rounds(act, PH_OL, o_lru, first_apart=True, last_apart=True)
            merged_hi([7])

            def wo(i):
                for c in range(4):
                    hi(PH_WO, i, c + LEAD)
                    if isinstance(i, int) and c % 2:
                        for k in range(4 * c - 4, 4 * c + 4):
                            act.wait_ge(mem_turned, k - k % 2 + 2)
                            act.activation(asp[:, k, 0:T], ps[:, 4 + (k // 2) % 4, (k % 2) * T:(k % 2 + 1) * T], ACT.Copy,
                                           scale=par[:, G_MEM + k:G_MEM + k + 1]).then_inc(mem_hi, 1)
                    if c % 2:
                        for e in range(2):
                            cross(PH_WO, i, c - 1 + e)
            wo(0)
            act.wait_ge(m_lo, KT // 2)
            act.dma_start(a_tok, x_tok).then_inc(x2_in, 16)
            with act.Fori(1, PH_WO.trips) as i:
                wo(i)

            def square(n, tile):
                act.wait_ge(ysq_done, KT + max(n - 1, 0))
                act.activation(ACS[n % 2], tile, ACT.Square).then_inc(sq_made, 1)

            def residual(k, g, base):
                act.wait_ge(res_out, base + k + 1)
                act.activation(hsp[:, k, 0:T], big_b[:, k, :], ACT.Copy,
                               scale=par[:, g + k:g + k + 1]).then_inc(res_hi, 1)

            for n, ph in enumerate((PH_CK, PH_CV)):
                for c in range(4):
                    hi(ph, 0, c + LEAD)
                    if c % 2:
                        for e in range(2):
                            cross(ph, 0, c - 1 + e)
                    if (n, c) == (0, 0):
                        root(4, RS, RV)
                    for k in range(*RES_AT.get((n, c), (0, 0))):
                        residual(k, G_PRE_X, 0)
                    if (n, c) == (1, 3):
                        for k in range(KT // 2):
                            square(k, big_b[:, k, :])
            for c in range(4):
                hi(PH_CQ, 0, c + LEAD)
                if c == 0:
                    for k in range(KT // 2, KT):
                        square(k, big_b[:, k, :])
                if c == 2:
                    for e in range(2):
                        cross(PH_CQ, 0, e)
            root(5, RS, RV)
            for e in range(2):
                cross(PH_CQ, 0, 2 + e)

            def x_exps(h):
                act.wait_ge(neg_max, HEADS + h + 1)
                for q in range(2):
                    act.activation(XP[h][:, q, :], ps[:, 4 + h, q * T:(q + 1) * T], ACT.Exp,
                                   bias=xst(h, 1)[:, q:q + 1], scale=XSCALE, accum_out=xst(h, 2)[:, q:q + 1]).then_inc(exps_done, 1)

            def x_copy(h):
                act.wait_ge(probs_turned, HEADS + h + 1)
                act.activation(XPT[h], ps[:, h, :].rearrange("p (m t) -> p m t", m=2), ACT.Copy).then_inc(probs_copied, 1)

            def co_hi(h):
                act.wait_ge(pv_done, HEADS // 2 + h + 1)
                act.activation(asp[:, h, 0:T], ps[:, 4 + h, 0:T], ACT.Copy).then_inc(o_hi, 1)
            for h in range(2):
                x_exps(h)
            for h in range(XH):
                x_copy(h)
                if h + 2 < XH:
                    x_exps(h + 2)
                if h:
                    co_hi(h - 1)
            co_hi(XH - 1)

            def co_square(t):
                act.wait_ge(tile_out, PH_CO.t(0, t) + 1)
                square(KT + t, big_a[:, t, :])
            for c in range(4):
                hi(PH_CO, 0, c + LEAD)
                for j in range(4):
                    cross(PH_CO, 0, 4 * c + j)
                    if 4 * c + j >= 2:
                        co_square(4 * c + j - 2)
            co_square(KT - 2)
            co_square(KT - 1)
            root(6, RS, RV)
            for k in range(KT):
                residual(k, G_PRE_FFN, KT)

            for n, ((f0, fn), up, dn) in enumerate(zip(GROUPS, PH_UP, PH_DN)):
                def up_round(i, first=False, split=False):
                    def bias(v):
                        for e in range(2):
                            act.wait_ge(up_ready, i * 4 + 2 * f0 + 2 * v + e + 1)
                            m = i * 2 + f0 + e + v * FT
                            act.activation(UC[2 * v + e], UR[2 * v + e], ACT.Identity, scale=col(W_F + 2 * P, m),
                                           bias=col(B_F, m)).then_inc(up_bias, 1)
                    if not split:
                        hi(up, i, 2)
                        hi(up, i, 3)
                    if first:
                        for k in range(KT // 2):
                            square(2 * KT + k, big_b[:, k, :])
                        hi(up, i, 4)
                        for k in range(KT // 2, KT):
                            square(2 * KT + k, big_b[:, k, :])
                    def pair(v):
                        for j in (2 * v, 2 * v + 1):
                            cross(up, i, j, scaled=None if first else i * 4 + 2 * f0 + j - 3)
                    pair(0)
                    if first:
                        hi(up, i, 5)
                        pair(1)
                        root(7, RS, RV)
                        hi(up, i, 6)
                        hi(up, i, 7)
                    bias(0)
                    if not first:
                        hi(up, i, 4)
                    for e in range(2):
                        act.wait_ge(up_conv, i * 4 + 2 * f0 + e + 1)
                        act.activation(UC[e], UC[e], ACT.Gelu_apprx_tanh).then_inc(gelu_done, 1)
                    if not first:
                        hi(up, i, 5)
                        pair(1)
                    bias(1)
                    for e in range(2):
                        act.wait_ge(hid_out, i * 2 + f0 + e + 1)
                        act.activation(asp[:, bass.ds(i * 2 + e, 1), 0:T].rearrange("p a t -> p (a t)"), HID[e],
                                       ACT.Copy).then_inc(hid_hi, 1)
                if n == 0:
                    up_round(0, first=True)
                    up_round(1, split=True)
                    with act.Fori(2, up.trips) as i:
                        up_round(i)
                else:
                    rounds(act, up, up_round)

                def dn_round(i):
                    for c in range(4):
                        hi(dn, i, c + LEAD)
                        cross(dn, i, c)
                rounds(act, dn, dn_round, last_apart=(n == len(GROUPS) - 1))
            root(8, RS, RV)
            for kq in range(4):
                for m in range(2):
                    act.wait_ge(fin_turned, 2 * kq + m + 1)
                    act.activation(out_sb[:, m, kq * 512:(kq + 1) * 512], ps[:, 2 * kq + m, :], ACT.Copy).then_inc(fin_copied, 1)

        @block.vector
        def _(dve):
            own = Tally(dve, dve_self)

            def lo(ph, i, c):
                p0 = ph.p0 + c
                if isinstance(i, int) and ph.p(i, c) >= PIECES:
                    return
                dve.wait_ge(hi_done, ph.p(i, c) + 1)
                n, slot = piece_size(ph, c), p0 % SLOTS
                dve.tensor_tensor(wsp[:, slot, 1, 0:n], raw[:, slot, 0:n], wsp[:, slot, 0, 0:n].bitcast(F32),
                                  ALU.subtract).then_inc(lo_done, 1)

            def add(ph, i, j, dst, slot=None, bank=None):
                slot = j % 4 if slot is None else slot
                bank = j % 4 if bank is None else bank
                dve.wait_ge(cross_done, ph.t(i, j) + 1)
                return dve.tensor_tensor(dst, ps[:, bank, 0:T], cr[:, slot, :], ALU.add)

            def tile_at(buf, m):
                return buf[:, bass.ds(m, 1), :].rearrange("p a t -> p (a t)")

            def small_rms(n, src_sem, count):
                dve.wait_ge(src_sem, count)
                dve.tensor_scalar(st[:, 2:4], st[:, 0:2], 1.0 / D, EPS, ALU.mult, ALU.add).then_inc(var_ready, 1)
                dve.wait_ge(root_ready, n)
                newton(st[:, 2:4], st[:, 4:6], st[:, 6:8], st[:, 26:28])

            def newton(v, root_, r0, r):
                own.link(dve.reciprocal(r0, root_))
                own.link(dve.tensor_tensor(r, r0, r0, ALU.mult))
                own.link(dve.tensor_tensor(r, r, v, ALU.mult))
                own.link(dve.tensor_scalar(r, r, -0.5, 1.5, ALU.mult, ALU.add))
                ins = dve.tensor_tensor(r, r, r0, ALU.mult)
                ins.then_inc(rms_ready, 1)
                rms_n[0] += 1
                dve.wait_ge(rms_ready, rms_n[0])
            rms_n = [0]

            def rms(n, sum_sem, count, bank, width):
                dve.wait_ge(sum_sem, count)
                dve.tensor_scalar(RV, ps[:, bank, 0:T], 1.0 / width, EPS, ALU.mult, ALU.add).then_inc(var_ready, 1)
                dve.wait_ge(root_ready, n)
                newton(RV, RS, RT0, RR)

            small_rms(1, x_sq, 2)
            dve.tensor_scalar(a_tok[:, 0, :], a_tok[:, 0, :], st[:, 26:27], None, ALU.mult).then_inc(x_scaled, 1)
            dve.wait_ge(par_turned, 6)
            dve.tensor_copy(par[:, 0:4 * P], ps[:, 4, :]).then_inc(par_ready, 1)
            dve.tensor_copy(par[:, 4 * P:6 * P], ps[:, 5, 0:2 * P]).then_inc(par_ready, 1)
            dve.wait_ge(par_ready, 2)
            lam = par[:, LAM:LAM + KT]
            dve.scalar_tensor_tensor(out=st[:, 32:48], in0=lam, scalar=-1.0, in1=lam, op0=ALU.mult, op1=ALU.max).then_inc(par_ready, 1)
            dve.tensor_scalar(lam, lam, -4.0, 0.0, ALU.mult, ALU.max).then_inc(par_ready, 1)
            for c in range(LEAD):
                lo(PH_A, 0, c)
            for k in range(KT):
                dve.wait_ge(x_hi, k - k % 2 + 2)
                dve.scalar_tensor_tensor(out=hsp[:, k, T:2 * T], in0=ps[:, k // 2, (k % 2) * T:(k % 2 + 1) * T],
                                         scalar=par[:, G_PRE_MIX + k:G_PRE_MIX + k + 1], in1=hsp[:, k, 0:T].bitcast(F32),
                                         op0=ALU.mult, op1=ALU.subtract).then_inc(x_lo, 1)
            for c in range(8):
                lo(PH_A, 0, c + LEAD)
                if c == 1:
                    e_, s_, s2, p_ = st[:, 48:64], st[:, 32:48], st[:, 64:80], st[:, 80:96]
                    dve.wait_ge(lam_exp, 1)
                    own.link(dve.tensor_scalar(s_, e_, 2.0, None, ALU.add))
                    own.link(dve.reciprocal(s_, s_))
                    own.link(dve.tensor_tensor(s_, s_, e_, ALU.mult))
                    own.link(dve.tensor_tensor(s2, s_, s_, ALU.mult))
                    own.link(dve.tensor_scalar(p_, s2, 1.0 / 17, None, ALU.mult))
                    for n in (15, 13, 11, 9, 7, 5, 3):
                        own.link(dve.scalar_tensor_tensor(out=p_, in0=p_, scalar=1.0 / n, in1=s2, op0=ALU.add, op1=ALU.mult))
                    own.link(dve.scalar_tensor_tensor(out=p_, in0=p_, scalar=1.0, in1=s_, op0=ALU.add, op1=ALU.mult))
                    own.link(dve.scalar_tensor_tensor(out=lam, in0=p_, scalar=8.0, in1=lam, op0=ALU.mult, op1=ALU.add))
                if c == 3:
                    dve.wait_ge(pos_in, 32)
                    own.link(dve.tensor_copy(COS, pos_i[:, :]))
                    own.link(dve.tensor_scalar(COS, COS, invf[:, 0:1], None, ALU.mult))
                    own.link(dve.tensor_scalar(SIN, COS, 1.0 / (2 * PI), MAGIC, ALU.mult, ALU.add))
                    own.link(dve.tensor_scalar(SIN, SIN, -MAGIC, None, ALU.add))
                    for part in TWO_PI:
                        own.link(dve.scalar_tensor_tensor(out=COS, in0=SIN, scalar=-part, in1=COS, op0=ALU.mult, op1=ALU.add))
                    own.link(dve.tensor_scalar(SIN, COS, 3.1415925, -3.1415925, ALU.min, ALU.max))
                    own.link(dve.scalar_tensor_tensor(out=COS, in0=SIN, scalar=-1.0, in1=SIN, op0=ALU.mult, op1=ALU.max))
                    dve.tensor_scalar(COS, COS, -1.0, PI / 2, ALU.mult, ALU.add).then_inc(angle_ready, 2)
            for j in range(RT):
                add(PH_A, 0, j, CKV[j], slot=(j + 3) % 4, bank=j).then_inc(tile_out, 1)
            dve.wait_ge(cross_done, 5)
            for to in (0, 64):
                ins = dve.tensor_tensor(KRAW[to:to + 64, :], ps[64:P, 4, 0:T], cr[64:P, 3, :], ALU.add)
            ins.then_inc(tile_out, 1)
            lo(PH_Q0, 0, 2)
            rms(2, ckv_sum, 1, 5, RANK)
            for j in range(RT):
                dve.tensor_tensor(CKV[j], CKV[j], RR, ALU.mult).then_inc(ckv_norm, 1)
            lo(PH_Q0, 0, 3)

            def rotate(n, dst, src):
                dve.wait_ge(rot_done, n)
                own.link(dve.tensor_tensor(ROTT, ps[:, 6, 0:T], SIN, ALU.mult))
                own.link(dve.tensor_tensor(dst, src, COS, ALU.mult))
                dve.tensor_tensor(dst, dst, ROTT, ALU.add).then_inc(roped, 1)
            dve.wait_ge(table_ready, 2)
            dve.wait_ge(tile_out, 5)
            rotate(1, KR, KRAW)
            for j in range(RT):
                dve.wait_ge(ckv_hi, j + 1)
                dve.scalar_tensor_tensor(out=asp[:, j, T:2 * T], in0=CKV[j], scalar=par[:, G_CKV + j:G_CKV + j + 1],
                                         in1=asp[:, j, 0:T].bitcast(F32), op0=ALU.mult, op1=ALU.subtract).then_inc(ckv_lo, 1)
            lo(PH_Q0, 0, 4)
            lo(PH_Q0, 0, 5)

            def q_out(ph, i):
                low, high = slice(0, 64), slice(64, P)
                moves = {1: [(low, QRAW, low), (high, QN[1], low)],
                         2: [(low, QN[1], high), (high, QRAW, high)]}
                for n, b in enumerate(Q_ORDER):
                    dve.wait_ge(cross_done, ph.t(i, n) + 1)
                    if b == 0:
                        ins = dve.tensor_tensor(QN[0], ps[:, b, 0:T], cr[:, n, :], ALU.add)
                    else:
                        for src, dst, to in moves[b]:
                            ins = dve.tensor_tensor(dst[to, :], ps[src, b, 0:T], cr[src, n, :], ALU.add)
                    ins.then_inc(tile_out, 1)
            q_out(PH_Q0, 0)

            def ukv(i):
                for c in range(4):
                    lo(PH_UKV, i, c + LEAD)
                    for j in range(2):
                        add(PH_UKV, i, 4 * c + j, tile_at(big_a, i * 8 + 2 * c + j)).then_inc(tile_out, 1)
                    for m in range(2):
                        add(PH_UKV, i, 4 * c + 2 + m, b_tok[:, m, bass.ds(i * 1024 + c * T, T)]).then_inc(tile_out, 1)
            rounds(dve, PH_UKV, ukv)

            def attention(u, ph, i, between, per=0):
                own.off = u * per
                lo(ph, i, 2)
                dve.wait_ge(tile_out, PH_Q.t(u, 0) - 1)
                rotate(u + 2, QROPE, QRAW)
                lo(ph, i, 3)
                for e in range(2):
                    dve.wait_ge(scores_done, u * 2 + e + 1)
                    own.link(dve.scalar_tensor_tensor(out=PR[e], in0=ps[:, 3 + e, 0:384], scalar=SCALE, in1=mask[:, :],
                                                      op0=ALU.mult, op1=ALU.add))
                    own.mark(dve.tensor_reduce(st[:, 8 + 2 * e:9 + 2 * e], PR[e][:, 0:P], AX, ALU.max))
                    own.link(dve.tensor_reduce(st[:, 9 + 2 * e:10 + 2 * e], PR[e][:, P:3 * P], AX, ALU.max))
                    dve.tensor_scalar(st[:, 12 + 2 * e:14 + 2 * e], st[:, 8 + 2 * e:10 + 2 * e], -1.0, None,
                                      ALU.mult).then_inc(neg_max, 1)
                for e in range(2):
                    dve.wait_ge(exps_done, u * 4 + 2 * e + 2)
                    dve.reciprocal(st[:, 20 + 2 * e:22 + 2 * e], st[:, 16 + 2 * e:18 + 2 * e]).then_inc(sums_inv, 1)
                between(0)
                lo(ph, i, 4)
                lo(ph, i, 5)
                between(1)
                dve.wait_ge(o_hi, u + 1)
                dve.tensor_tensor(asp[:, bass.ds(u * 2, 2), T:2 * T], ps[:, 6, :].rearrange("p (e t) -> p e t", e=2),
                                  asp[:, bass.ds(u * 2, 2), 0:T].bitcast(F32), ALU.subtract).then_inc(o_lo, 1)
            n0 = own.n
            dve.wait_ge(mask_made, 2)
            rounds(dve, PH_Q, lambda i: attention(i, PH_Q, i, lambda part: part and q_out(PH_Q, i), 8))
            assert own.n == n0 + 8
            own.n, own.off = n0 + 8 * PH_Q.trips, 0

            def gm_tiles(i, part):
                for e in range(2):
                    add(PH_GM, i, 2 * part + e, tile_at(big_a, i * 4 + 2 * part + e)).then_inc(tile_out, 1)
            attention(HEADS // 2 - 1, PH_GM, 0, lambda part: gm_tiles(0, part))
            with dve.Fori(1, PH_GM.trips) as i:
                for part in range(2):
                    lo(PH_GM, i, 2 * part + 2)
                    lo(PH_GM, i, 2 * part + 3)
                    gm_tiles(i, part)
            small_rms(3, mem_sq, 2)
            for m in range(2):
                dve.tensor_scalar(b_tok[:, m, :], b_tok[:, m, :], st[:, 26 + m:27 + m], None, ALU.mult).then_inc(mem_scaled, 1)
            dve.wait_ge(gate_done, KT)
            n0 = own.n

            def om(i):
                own.n, own.off = n0, i * 4
                for c in range(4):
                    lo(PH_OM, i, c + LEAD)
                    if c % 2:
                        for e in range(2):
                            own.mark(add(PH_OM, i, c - 1 + e, cr[:, c - 1 + e, :]))
                        for e in range(2):
                            dve.wait_ge(dve_self, own.now() - 1 + e)
                            g = tile_at(big_a, i * 4 + c - 1 + e)
                            dve.tensor_tensor(g, g, cr[:, c - 1 + e, :], ALU.mult).then_inc(tile_out, 1)
            rounds(dve, PH_OM, om)
            own.n, own.off = n0 + 4 * PH_OM.trips, 0
            n0 = own.n

            def lru(i):
                ph = PH_LRU
                own.n, own.off = n0, i * 8
                lo(ph, i, 2)
                lo(ph, i, 3)
                for e in range(2):
                    add(ph, i, e, XR[e]).then_inc(tile_out, 1)
                for e in range(2):
                    dve.wait_ge(tile_out, ph.t(i, e) + 1)
                    own.mark(dve.tensor_scalar(XC[e], XR[e], par[:, bass.ds(i * 2 + W_CONV + 48 + e, 1)],
                                               par[:, bass.ds(i * 2 + B_CONV + e, 1)], ALU.mult, ALU.add))
                for d in (1, 2, 3):
                    for e in range(2):
                        dve.wait_ge(dve_self, own.now() - 1 + (e if d == 3 else 0))
                        ins = dve.scalar_tensor_tensor(out=XC[e][:, d:T], in0=XR[e][:, 0:T - d],
                                                       scalar=par[:, bass.ds(i * 2 + W_CONV + 16 * (3 - d) + e, 1)],
                                                       in1=XC[e][:, d:T], op0=ALU.mult, op1=ALU.add)
                        if d == 3:
                            ins.then_inc(conv_done, 1)
                        else:
                            own.mark(ins)
                if not isinstance(i, int) or i:
                    y_lo(i - 1)
                lo(ph, i, 4)
                for e in range(2):
                    dve.wait_ge(lru_t, i * 2 + e + 1)
                    own.mark(dve.tensor_scalar(RC[e], TH[e], 1.0, None, ALU.add))
                for e in range(2):
                    dve.wait_ge(dve_self, own.now() - 1 + e)
                    dve.reciprocal(RC[e], RC[e]).then_inc(lru_rc, 1)
                lo(ph, i, 5)
                for e in range(2):
                    add(ph, i, 2 + e, YY[e]).then_inc(tile_out, 1)
                for e in range(2):
                    dve.wait_ge(lru_a, i * 2 + e + 1)
                    dve.tensor_tensor_scan(TH[e], RC[e], SQT[e], 0.0, ALU.mult, ALU.add).then_inc(lru_scan, 1)
                assert own.n == n0 + 8

            def y_lo(i):
                for e in range(2):
                    dve.wait_ge(hrg_hi, i * 2 + e + 1)
                    m = asp[:, bass.ds(i * 2 + e, 1), :].rearrange("p a t -> p (a t)")
                    dve.tensor_tensor(m[:, T:2 * T], YY[e], m[:, 0:T].bitcast(F32), ALU.subtract).then_inc(hrg_lo, 1)
            rounds(dve, PH_LRU, lru, first_apart=True)
            own.n, own.off = n0 + 8 * PH_LRU.trips, 0

            def merged_lo(pairs):
                for k in pairs:
                    dve.wait_ge(m_hi, k + 1)
                    dve.tensor_tensor(hsp[:, 2 * k:2 * k + 2, T:2 * T], big_a[:, 2 * k:2 * k + 2, :],
                                      hsp[:, 2 * k:2 * k + 2, 0:T].bitcast(F32), ALU.subtract).then_inc(m_lo, 1)

            def o_lru(i):
                first, last = (isinstance(i, int) and i == n for n in (0, PH_OL.trips - 1))
                for c in range(4):
                    lo(PH_OL, i, c + LEAD)
                    if first and c == 0:
                        y_lo(PH_LRU.trips - 1)
                    if last and c >= 2:
                        merged_lo(range(4) if c == 2 else range(4, 7))
                    if c % 2:
                        if not first:
                            dve.wait_ge(merged_out, i * 2)
                        for e in range(2):
                            add(PH_OL, i, c - 1 + e, (OL_G if c == 1 else OL_O)[e]).then_inc(tile_out, 1)
            rounds(dve, PH_OL, o_lru, first_apart=True, last_apart=True)
            merged_lo([7])

            def wo(i):
                for c in range(4):
                    lo(PH_WO, i, c + LEAD)
                    if isinstance(i, int) and c % 2:
                        for k in range(4 * c - 4, 4 * c + 4):
                            dve.wait_ge(mem_hi, k - k % 2 + 2)
                            dve.scalar_tensor_tensor(out=asp[:, k, T:2 * T], in0=ps[:, 4 + (k // 2) % 4, (k % 2) * T:(k % 2 + 1) * T],
                                                     scalar=par[:, G_MEM + k:G_MEM + k + 1], in1=asp[:, k, 0:T].bitcast(F32),
                                                     op0=ALU.mult, op1=ALU.subtract).then_inc(mem_lo, 1)
                    if c % 2:
                        for e in range(2):
                            add(PH_WO, i, c - 1 + e, tile_at(big_b, i * 4 + c - 1 + e)).then_inc(tile_out, 1)
            wo(0)
            with dve.Fori(1, PH_WO.trips) as i:
                wo(i)

            def residual(k, g_post, base, xt):
                dve.wait_ge(y_scaled, base + k + 1)
                b = big_b[:, k, :]
                if xt:
                    dve.wait_ge(xt_turned, k + 1)
                    dve.scalar_tensor_tensor(out=b, in0=b, scalar=par[:, g_post + k:g_post + k + 1],
                                             in1=ps[:, 5 + k % 3, 0:T], op0=ALU.mult, op1=ALU.add).then_inc(res_out, 1)
                else:
                    dve.scalar_tensor_tensor(out=b, in0=big_a[:, k, :], scalar=par[:, g_post + k:g_post + k + 1],
                                             in1=b, op0=ALU.mult, op1=ALU.add).then_inc(res_out, 1)

            def residual_lo(k, g_pre, base):
                dve.wait_ge(res_hi, base + k + 1)
                dve.scalar_tensor_tensor(out=hsp[:, k, T:2 * T], in0=big_b[:, k, :], scalar=par[:, g_pre + k:g_pre + k + 1],
                                         in1=hsp[:, k, 0:T].bitcast(F32), op0=ALU.mult, op1=ALU.subtract).then_inc(res_lo, 1)

            for n, ph in enumerate((PH_CK, PH_CV)):
                for c in range(4):
                    lo(ph, 0, c + LEAD)
                    if c % 2:
                        for e in range(2):
                            j = c - 1 + e
                            dst = CKT[j] if n == 0 else CVT[:, e, (c // 2) * T:(c // 2 + 1) * T]
                            add(ph, 0, j, dst).then_inc(tile_out, 1)
                    if (n, c) == (0, 0):
                        rms(4, norm_sum, 1, 4, D)
                    for k in range(*RES_AT.get((n, c), (0, 0))):
                        residual(k, G_POST_MIX, 0, True)
                        if k:
                            residual_lo(k - 1, G_PRE_X, 0)
                        if k == KT - 1:
                            residual_lo(k, G_PRE_X, 0)
            for c in range(4):
                lo(PH_CQ, 0, c + LEAD)
            rms(5, norm_sum, 2, 4, D)
            for j in range(XH):
                own.link(add(PH_CQ, 0, j, cr[:, j, :]))
                dve.tensor_tensor(CQ[j], cr[:, j, :], RR, ALU.mult).then_inc(tile_out, 1)

            def x_max(h):
                dve.wait_ge(scores_done, HEADS + h + 1)
                own.link(dve.tensor_reduce(xst(h, 0), ps[:, 4 + h, :].rearrange("p (q t) -> p q t", q=2), AX, ALU.max))
                dve.tensor_scalar(xst(h, 1), xst(h, 0), -XSCALE, None, ALU.mult).then_inc(neg_max, 1)

            def x_norm(h):
                dve.wait_ge(exps_done, 2 * HEADS + 2 * h + 2)
                own.link(dve.reciprocal(xst(h, 3), xst(h, 2)))
                for q in range(2):
                    blk = XP[h][:, q, :]
                    dve.tensor_scalar(blk, blk, xst(h, 3)[:, q:q + 1], None, ALU.mult).then_inc(probs_ready, 1)

            def co_lo(h):
                dve.wait_ge(o_hi, HEADS // 2 + h + 1)
                dve.tensor_tensor(asp[:, h, T:2 * T], ps[:, 4 + h, 0:T], asp[:, h, 0:T].bitcast(F32), ALU.subtract).then_inc(o_lo, 1)
            for h in range(2):
                x_max(h)
            for h in range(XH):
                x_norm(h)
                if h + 2 < XH:
                    x_max(h + 2)
            for h in range(XH):
                co_lo(h)
            for c in range(4):
                lo(PH_CO, 0, c + LEAD)
                for j in range(4):
                    add(PH_CO, 0, 4 * c + j, big_a[:, 4 * c + j, :]).then_inc(tile_out, 1)
            rms(6, norm_sum, 3, 4, D)
            for k in range(KT + 1):
                if k < KT:
                    residual(k, G_POST_X, KT, False)
                if k:
                    residual_lo(k - 1, G_PRE_FFN, KT)

            for n, ((f0, fn), up, dn) in enumerate(zip(GROUPS, PH_UP, PH_DN)):
                n0 = own.n

                def up_round(i, first=False, split=False):
                    def sums(v):
                        for j in (2 * v, 2 * v + 1):
                            add(up, i, j, cr[:, j, :]).then_inc(tile_out, 1)

                    def unit(v):
                        for e in range(2):
                            dve.wait_ge(tile_out, up.t(i, 2 * v + e) + 1)
                            dve.tensor_tensor(UR[2 * v + e], cr[:, 2 * v + e, :], RR, ALU.mult).then_inc(up_ready, 1)
                        for e in range(2):
                            m = i * 2 + f0 + e + v * FT
                            dve.wait_ge(up_bias, i * 4 + 2 * f0 + 2 * v + e + 1)
                            buf, src = UC[2 * v + e], UR[2 * v + e]
                            own.mark(dve.scalar_tensor_tensor(out=buf[:, 1:T], in0=src[:, 0:T - 1], scalar=col(W_F + P, m),
                                                              in1=buf[:, 1:T], op0=ALU.mult, op1=ALU.add))
                        for e in range(2):
                            m = i * 2 + f0 + e + v * FT
                            dve.wait_ge(dve_self, own.now() - 1 + e)
                            buf, src = UC[2 * v + e], UR[2 * v + e]
                            dve.scalar_tensor_tensor(out=buf[:, 2:T], in0=src[:, 0:T - 2], scalar=col(W_F, m),
                                                     in1=buf[:, 2:T], op0=ALU.mult, op1=ALU.add).then_inc(up_conv, 1)
                    if first:
                        for c in (2, 3, 4):
                            lo(up, i, c)
                        sums(0)
                        lo(up, i, 5)
                        sums(1)
                        rms(7, norm_sum, 4, 4, D)
                        base[0] = own.n
                    own.n, own.off = base[0], i * 4
                    if not first and not split:
                        lo(up, i, 2)
                        lo(up, i, 3)
                    if not first:
                        sums(0)
                    unit(0)
                    if first:
                        lo(up, i, 6)
                        lo(up, i, 7)
                    else:
                        lo(up, i, 4)
                        lo(up, i, 5)
                        sums(1)
                    unit(1)
                    for e in range(2):
                        dve.wait_ge(hid_hi, i * 2 + f0 + e + 1)
                        m = asp[:, bass.ds(i * 2 + e, 1), :].rearrange("p a t -> p (a t)")
                        dve.tensor_tensor(m[:, T:2 * T], HID[e], m[:, 0:T].bitcast(F32), ALU.subtract).then_inc(hid_lo, 1)
                    assert own.n == base[0] + 4
                base = [own.n]
                if n == 0:
                    up_round(0, first=True)
                    up_round(1, split=True)
                    with dve.Fori(2, up.trips) as i:
                        up_round(i)
                else:
                    rounds(dve, up, up_round)
                own.n, own.off = base[0] + 4 * up.trips, 0
                n0d = own.n

                def dn_round(i):
                    own.n, own.off = n0d, i * 4
                    for c in range(4):
                        lo(dn, i, c + LEAD)
                        y = tile_at(big_a, i * 4 + c)
                        if n == 0:
                            add(dn, i, c, y).then_inc(tile_out, 1)
                        else:
                            own.link(add(dn, i, c, cr[:, c, :]))
                            dve.tensor_tensor(y, y, cr[:, c, :], ALU.add).then_inc(tile_out, 1)
                rounds(dve, dn, dn_round, last_apart=(n == len(GROUPS) - 1))
                if n:
                    own.n = n0d + 4 * dn.trips
                own.off = 0
            rms(8, norm_sum, 5, 4, D)
            for k in range(0, KT, 2):
                own.link(dve.tensor_tensor(big_a[:, k, :], big_a[:, k, :], RR, ALU.mult))
                for j in (k, k + 1):
                    if j % 2:
                        dve.wait_ge(y_scaled, 2 * KT + j // 2 + 1)
                    dve.scalar_tensor_tensor(out=big_b[:, j, :], in0=big_a[:, j, :], scalar=par[:, G_POST_FFN + j:G_POST_FFN + j + 1],
                                             in1=big_b[:, j, :], op0=ALU.mult, op1=ALU.add).then_inc(res_out, 1)

        @block.gpsimd
        def _(pool):
            own = Tally(pool, pool_self)
            pool.memset(scr[:, 0:6 * P], 0.0).then_inc(prow_zero, 1)
            own.mark(pool.memset(ident[:, :], 0.0))
            own.mark(pool.memset(rotm[:, :], 0.0))
            own.link(pool.memset(mask[:, :], 0.0))
            pool.memset(ones[:, :], 1.0).then_inc(consts_made, 1)
            pool.affine_select(out=ident[:, :], in_=ident[:, :], compare_op=ALU.not_equal, fill=1.0, base=0,
                               pattern=[[-1, P]], channel_multiplier=1).then_inc(consts_made, 1)
            rv = rotm[:, :].rearrange("p (g h j) -> p g h j", g=2, h=2)
            for h, fill in ((0, -1.0), (1, 1.0)):
                ins = pool.affine_select(out=rv[:, :, h, :], in_=rv[:, :, h, :], compare_op=ALU.not_equal, fill=fill,
                                         base=-32 if h == 0 else 0, pattern=[[-64, 2], [-1, 32]], channel_multiplier=1)
                ins.then_inc(consts_made, 1)
            for q in range(2):
                blk = mask[:, 2 * q * P:(2 * q + 1) * P]
                ins = pool.affine_select(out=blk, in_=blk, compare_op=ALU.is_ge, fill=NEG, base=0, pattern=[[-1, P]],
                                         channel_multiplier=1)
                ins.then_inc(mask_made, 1)

            def attention(u):
                if not isinstance(u, int):
                    pool.wait_ge(pv_done, u)
                pool.tensor_copy(cur[:, :].rearrange("p (e t) -> p e t", e=2), big_a[:, bass.ds(u * 2, 2), :]).then_inc(kv_cur, 1)
                pool.tensor_copy(scr[:, 768:1280].rearrange("p (m d) -> p m d", m=2), b_tok[:, :, bass.ds(u * T, T)]).then_inc(kv_cur, 1)
                for e in range(2):
                    pool.wait_ge(sums_inv, u * 2 + e + 1)
                    for q in range(2):
                        n = 2 * e + q
                        blk = PR[e][:, P * q:P * q + P * (q + 1)]
                        inv = st[:, 20 + n:21 + n].to_broadcast([P, P * (q + 1)])
                        pool.tensor_tensor(blk, blk, inv, ALU.mult).then_inc(probs_ready, 1)
            pool.wait_ge(tile_out, PH_UKV.t_end)
            attention(0)
            with pool.Fori(1, HEADS // 2) as u:
                attention(u)

            n0 = own.n

            def y_mult(i):
                for e in range(2):
                    pool.wait_ge(y_act, i * 2 + e + 1)
                    pool.wait_ge(lru_scan, i * 2 + e + 1)
                    pool.tensor_tensor(YY[e], YY[e], TH[e], ALU.mult).then_inc(hrg, 1)

            def lru(i):
                own.n, own.off = n0, i * 6
                if not isinstance(i, int) or i:
                    y_mult(i - 1)
                for e in range(2):
                    pool.wait_ge(gates_act, i * 4 + 2 * e + 2)
                    own.mark(pool.tensor_tensor(IG[e], IG[e], XC[e], ALU.mult))
                    pool.wait_ge(lru_root, i * 2 + e + 1)
                    pool.wait_ge(lru_rc, i * 2 + e + 1)
                    own.mark(pool.tensor_tensor(SQT[e], SQT[e], RC[e], ALU.mult))
                    own.link(pool.tensor_scalar(RC[e], RC[e], 2.0, -1.0, ALU.mult, ALU.add))
                    pool.tensor_tensor(SQT[e], SQT[e], IG[e], ALU.mult).then_inc(lru_a, 1)
                assert own.n == n0 + 6
            rounds(pool, PH_LRU, lru, first_apart=True)
            y_mult(PH_LRU.trips - 1)
            own.n, own.off = n0 + 6 * PH_LRU.trips, 0
            n1 = own.n

            def o_lru(i):
                own.n, own.off = n1, i * 2
                for e in range(2):
                    pool.wait_ge(olg_sig, i * 2 + e + 1)
                    pool.wait_ge(tile_out, PH_OL.t(i, 2 + e) + 1)
                    own.link(pool.tensor_tensor(OL_O[e], OL_O[e], OL_G[e], ALU.mult))
                    g = big_a[:, bass.ds(i * 2 + e, 1), :].rearrange("p a t -> p (a t)")
                    pool.tensor_tensor(g, g, OL_O[e], ALU.add).then_inc(merged_out, 1)
            rounds(pool, PH_OL, o_lru)
            own.n, own.off = n1 + 2 * PH_OL.trips, 0

            def add_square(tile_done, y, count, e):
                pool.wait_ge(tile_out, tile_done + 1)
                own.link(pool.tensor_tensor(ACS[e], y, y, ALU.mult))
                if not isinstance(count, int) or count:
                    pool.wait_ge(ysq_done, count)
                pool.tensor_tensor(ACC, ACC, ACS[e], ALU.add).then_inc(ysq_done, 1)

            own.link(pool.memset(ACC, 0.0))
            n2 = own.n

            def wo(i):
                own.n, own.off = n2, i * 4
                for j in range(4):
                    y = big_b[:, bass.ds(i * 4 + j, 1), :].rearrange("p a t -> p (a t)")
                    add_square(PH_WO.t(i, j), y, i * 4 + j, j % 2)
            rounds(pool, PH_WO, wo, first_apart=True)
            own.n, own.off = n2 + 4 * PH_WO.trips, 0

            def add_made(n):
                pool.wait_ge(sq_made, n + 1)
                pool.wait_ge(ysq_done, KT + n)
                pool.tensor_tensor(ACC, ACC, ACS[n % 2], ALU.add).then_inc(ysq_done, 1)

            def scale_tiles(buf, n_rms, tiles=range(KT)):
                pool.wait_ge(rms_ready, n_rms)
                for k in tiles:
                    pool.tensor_tensor(buf[:, k, :], buf[:, k, :], RR, ALU.mult).then_inc(y_scaled, 1)

            def new_sum(count):
                pool.wait_ge(norm_sum, count)
                own.link(pool.memset(ACC, 0.0))

            new_sum(1)
            scale_tiles(big_b, 4)
            for n in range(KT):
                add_made(n)
            new_sum(2)
            for n in range(KT):
                add_made(KT + n)
            new_sum(3)
            scale_tiles(big_a, 6)
            for n in range(KT):
                add_made(2 * KT + n)

            for (f0, fn), up in zip(GROUPS, PH_UP):
                def up_round(i):
                    for e in range(2):
                        done = i * 2 + f0 + e
                        pool.wait_ge(gelu_done, done + 1)
                        pool.wait_ge(up_conv, i * 4 + 2 * f0 + 2 + e + 1)
                        if not isinstance(i, int) or f0:
                            pool.wait_ge(hid_lo, i * 2 + f0)
                        pool.tensor_tensor(HID[e], UC[e], UC[2 + e], ALU.mult).then_inc(hid_out, 1)
                rounds(pool, up, up_round, first_apart=(f0 == 0))
            own.link(pool.memset(ACC, 0.0))
            n3, dn = own.n, PH_DN[-1]

            def dn_round(i):
                own.n, own.off = n3, i * 4
                for j in range(4):
                    y = big_a[:, bass.ds(i * 4 + j, 1), :].rearrange("p a t -> p (a t)")
                    add_square(dn.t(i, j), y, i * 4 + 4 * KT + j, j % 2)
            rounds(pool, dn, dn_round)
            own.n, own.off = n3 + 4 * dn.trips, 0
            scale_tiles(big_a, 8, range(1, KT, 2))


NAMES = ["x", "mem", "positions", "g_pre_mix", "g_post_mix", "w_in", "g_ckv", "w_ukv", "w_o_mla", "w_conv_lru",
         "b_conv_lru", "w_rg", "b_rg", "w_ig", "b_ig", "lru_lambda", "w_o_lru", "w_out", "g_pre_x", "g_post_x",
         "g_mem", "w_cq", "w_ck", "w_cv", "w_co", "g_pre_ffn", "g_post_ffn", "w_up", "w_fconv", "b_fconv", "w_down"]


def kernel(**inputs):
    import numpy as np
    import concourse.bacc as bacc
    from concourse.bass_utils import run_bass_kernel_spmd

    nc = bacc.Bacc("TRN2", target_bir_lowering=False, num_devices=1, dynamic_dma_scratch_size=1024)
    arrays = {name: np.ascontiguousarray(inputs[name]) for name in NAMES}
    freq = np.float32(10000.0) ** (-np.arange(0, ROPE, 2, dtype=np.float32) / np.float32(ROPE))
    arrays["inv_freq"] = np.tile(freq.astype(np.float32), 4).reshape(P, 1)
    aps = {name: nc.dram_tensor(f"in_{name}", v.shape, mybir.dt.from_np(v.dtype), kind="ExternalInput").ap()
           for name, v in arrays.items()}
    out = nc.dram_tensor("out", (1, T, D), F32, kind="ExternalOutput").ap()
    build(nc, aps, out)
    r = run_bass_kernel_spmd(nc, [{f"in_{name}": v for name, v in arrays.items()}], core_ids=[0])
    return r.results[0]["out"]
```
